# Optimizing a Trainium2 kernel written in Bass

```python
import math
import jax, jax.numpy as jnp
from jax import lax
import numpy as np

D_MODEL = 1024
BATCH = 1
SEQ = 1024
DEPTH = 1
DEC_BATCH = 8
DEC_SEQ = 8
PAST_LEN = 4096
PAGE_SIZE = 128

HEAD_DIM = 64
ROT_DIM = HEAD_DIM // 4
ROPE_THETA = 500000.0
ATTN_SCALE = HEAD_DIM ** -0.5
RMS_EPS = 1e-6
Q_BLOCK = 128
A_HEADS = D_MODEL // (2 * HEAD_DIM)
A_QK = 2 * HEAD_DIM
A_V = 2 * HEAD_DIM
A_WIDTH = A_HEADS * A_V
DIL_PATTERNS = ((128, 1), (512, 4), (2048, 16))
N_GROUPS = len(DIL_PATTERNS)
B_HEADS = 4
B_WIDTH = B_HEADS * HEAD_DIM
DIL_KEYS = DIL_PATTERNS[0][0] // DIL_PATTERNS[0][1]
IN_A = 3 * A_HEADS * A_QK
IN_B = 3 * N_GROUPS * B_HEADS * HEAD_DIM
IN_G = 2 * D_MODEL
IN_TOTAL = IN_A + IN_B + IN_G
FFN_HIDDEN = -(-(8 * D_MODEL) // (3 * 256)) * 256

kernel_name = 'hybrid_diffattn_dilated_decoder_step'

def rmsnorm(x, g):
    xf = x.astype(jnp.float32)
    y = xf * lax.rsqrt(jnp.mean(xf * xf, axis=-1, keepdims=True) + RMS_EPS)
    return (y * g.astype(jnp.float32)).astype(x.dtype)

def rope_partial(x, pos):
    half = ROT_DIM // 2
    inv_freq = jnp.power(jnp.float32(ROPE_THETA), -jnp.arange(half, dtype=jnp.float32) * (2.0 / ROT_DIM))
    ang = pos.astype(jnp.float32)[:, None] * inv_freq[None, :]
    shape = (pos.shape[0],) + (1,) * (x.ndim - 3) + (half,)
    cos = jnp.cos(ang).reshape(shape)
    sin = jnp.sin(ang).reshape(shape)
    xf = x.astype(jnp.float32)
    x1, x2, rest = xf[..., :half], xf[..., half:ROT_DIM], xf[..., ROT_DIM:]
    out = jnp.concatenate([x1 * cos - x2 * sin, x2 * cos + x1 * sin, rest], axis=-1)
    return out.astype(x.dtype)

def project(h, w_in, pos):
    n, s, _ = h.shape
    z = h @ w_in
    za = z[..., :IN_A].reshape(n, s, 3, A_HEADS, 2, HEAD_DIM)
    zb = z[..., IN_A:IN_A + IN_B].reshape(n, s, 3, N_GROUPS, B_HEADS, HEAD_DIM)
    zg = z[..., IN_A + IN_B:]
    qa = rope_partial(za[:, :, 0], pos)
    ka = rope_partial(za[:, :, 1], pos)
    va = za[:, :, 2].reshape(n, s, A_HEADS, A_V)
    qb = rope_partial(zb[:, :, 0], pos)
    kb = rope_partial(zb[:, :, 1], pos)
    vb = zb[:, :, 2]
    return qa, ka, va, qb, kb, vb, zg[..., :D_MODEL], zg[..., D_MODEL:]

def diff_attn_prompt(q, k, v, lam):
    n, s = q.shape[:2]
    nb = s // Q_BLOCK
    kpos = jnp.arange(s)
    vf = v.astype(jnp.float32)
    qblocks = jnp.moveaxis(q.reshape(n, nb, Q_BLOCK, A_HEADS, 2, HEAD_DIM), 1, 0)

    def one_block(args):
        blk, qb = args
        qpos = blk * Q_BLOCK + jnp.arange(Q_BLOCK)
        mask = kpos[None, :] <= qpos[:, None]
        sc = jnp.einsum('bqhce,bkhce->bchqk', qb, k).astype(jnp.float32) * ATTN_SCALE
        p = jax.nn.softmax(jnp.where(mask, sc, -jnp.inf), axis=-1)
        a = p[:, 0] - lam * p[:, 1]
        return jnp.einsum('bhqk,bkhe->bqhe', a, vf)

    o = lax.map(one_block, (jnp.arange(nb), qblocks))
    return jnp.moveaxis(o, 0, 1).reshape(n, s, A_HEADS, A_V)

def diff_attn_sample(q, k, v, k_past, v_past, lam):
    t = q.shape[1]
    npast = k_past.shape[1]
    causal = jnp.tril(jnp.ones((t, t), dtype=bool))
    s_past = jnp.einsum('bqhce,bkhce->bchqk', q, k_past).astype(jnp.float32)
    s_new = jnp.einsum('bqhce,bkhce->bchqk', q, k).astype(jnp.float32)
    s_new = jnp.where(causal, s_new, -jnp.inf)
    p = jax.nn.softmax(jnp.concatenate([s_past, s_new], axis=-1) * ATTN_SCALE, axis=-1)
    a = p[:, 0] - lam * p[:, 1]
    return (jnp.einsum('bhqk,bkhe->bqhe', a[..., :npast], v_past.astype(jnp.float32))
            + jnp.einsum('bhqk,bkhe->bqhe', a[..., npast:], v.astype(jnp.float32)))

def diff_finish(o, subln_w, lam_init, dtype):
    n, s = o.shape[:2]
    y = o * lax.rsqrt(jnp.mean(o * o, axis=-1, keepdims=True) + RMS_EPS) * subln_w.astype(jnp.float32)
    return (y * (1.0 - lam_init)).reshape(n, s, A_WIDTH).astype(dtype)

def dilated_attn_prompt(q, k, v, dil):
    n, s, h, e = q.shape
    L = s // dil
    nblk = -(-L // DIL_KEYS)
    lp = nblk * DIL_KEYS

    def to_sub(x):
        x = jnp.transpose(x.reshape(n, L, dil, h, e), (0, 2, 1, 3, 4))
        return jnp.pad(x, ((0, 0), (0, 0), (0, lp - L), (0, 0), (0, 0)))

    def band(x):
        xp = jnp.pad(to_sub(x), ((0, 0), (0, 0), (DIL_KEYS, 0), (0, 0), (0, 0)))
        xp = xp.reshape(n, dil, nblk + 1, DIL_KEYS, h, e)
        return jnp.concatenate([xp[:, :, :-1], xp[:, :, 1:]], axis=3)

    qs = to_sub(q).reshape(n, dil, nblk, DIL_KEYS, h, e)
    kb, vb = band(k), band(v)
    sc = jnp.einsum('bdnqhe,bdnkhe->bdnhqk', qs, kb).astype(jnp.float32) * ATTN_SCALE
    qi = jnp.arange(DIL_KEYS)[:, None]
    kj = jnp.arange(2 * DIL_KEYS)[None, :]
    dist = qi + DIL_KEYS - kj
    kpos = jnp.arange(nblk)[:, None, None] * DIL_KEYS - DIL_KEYS + kj[None]
    mask = (dist >= 0) & (dist <= DIL_KEYS) & (kpos >= 0)
    sc = jnp.where(mask[:, None], sc, -jnp.inf)
    m = jnp.max(sc, axis=-1, keepdims=True)
    p = jnp.exp(sc - m)
    den = jnp.sum(p, axis=-1, keepdims=True)
    o = jnp.einsum('bdnhqk,bdnkhe->bdnqhe', p / den, vb.astype(jnp.float32))
    lse = jnp.swapaxes((m + jnp.log(den))[..., 0], 3, 4)
    o = jnp.transpose(o.reshape(n, dil, lp, h, e)[:, :, :L], (0, 2, 1, 3, 4)).reshape(n, s, h, e)
    lse = jnp.transpose(lse.reshape(n, dil, lp, h)[:, :, :L], (0, 2, 1, 3)).reshape(n, s, h)
    return o, lse

def dilated_attn_sample(q, k, v, buf, dil):
    t = q.shape[1]
    keep = buf.shape[1]
    kc = jnp.concatenate([buf[:, :, 0], k], axis=1)
    vc = jnp.concatenate([buf[:, :, 1], v], axis=1)
    idx = keep + jnp.arange(t)[:, None] - dil * jnp.arange(DIL_KEYS + 1)[None, :]
    valid = idx >= 0
    idx = jnp.maximum(idx, 0)
    kg = kc[:, idx]
    vg = vc[:, idx]
    sc = jnp.einsum('bthe,btjhe->bhtj', q, kg).astype(jnp.float32) * ATTN_SCALE
    sc = jnp.where(valid, sc, -jnp.inf)
    m = jnp.max(sc, axis=-1, keepdims=True)
    p = jnp.exp(sc - m)
    den = jnp.sum(p, axis=-1, keepdims=True)
    o = jnp.einsum('bhtj,btjhe->bthe', p / den, vg.astype(jnp.float32))
    lse = jnp.swapaxes((m + jnp.log(den))[..., 0], 1, 2)
    new_buf = jnp.stack([kc[:, t:], vc[:, t:]], axis=2)
    return o, lse, new_buf

def combine_groups(outs, lses):
    o = jnp.stack(outs, axis=0)
    w = jax.nn.softmax(jnp.stack(lses, axis=0), axis=0)
    y = jnp.sum(w[..., None] * o, axis=0)
    n, s = y.shape[:2]
    return y.reshape(n, s, B_WIDTH)

def merge_branches(x, oa, ob, ga, gb, w_b_up, w_out, post_g):
    m = jax.nn.sigmoid(ga) * oa + jax.nn.sigmoid(gb) * (ob.astype(x.dtype) @ w_b_up)
    return x + rmsnorm(m @ w_out, post_g)

def swiglu_ffn(x, pre_g, w_gu, w_down, post_g):
    u = rmsnorm(x, pre_g) @ w_gu
    y = (jax.nn.silu(u[..., :FFN_HIDDEN]) * u[..., FFN_HIDDEN:]) @ w_down
    return x + rmsnorm(y, post_g)

def setup_inputs(seed: int = 0) -> dict:
    key = jax.random.key(seed)
    ks = jax.random.split(key, 22)
    f32 = jnp.float32
    n_pages = PAST_LEN // PAGE_SIZE
    n_used = DEC_BATCH * n_pages
    n_pool = (5 * n_used + 3) // 4

    def nrm(k, shape, scale=1.0):
        return jax.random.normal(k, shape, f32) * scale

    def gain(k, n):
        return 1.0 + 0.05 * jax.random.normal(k, (DEPTH, n), f32)

    page_table = jax.random.permutation(ks[4], n_pool)[:n_used].reshape(DEC_BATCH, n_pages).astype(jnp.int32)
    wins = [nrm(ks[5 + g], (DEPTH, DEC_BATCH, min(w, PAST_LEN), 2, B_HEADS, HEAD_DIM))
            for g, (w, _) in enumerate(DIL_PATTERNS)]
    return {
        'x_prompt': nrm(ks[0], (BATCH, SEQ, D_MODEL)),
        'x_sample': nrm(ks[1], (DEC_BATCH, DEC_SEQ, D_MODEL)),
        'cache_k': nrm(ks[2], (DEPTH, n_pool, PAGE_SIZE, A_HEADS, A_QK)),
        'cache_v': nrm(ks[3], (DEPTH, n_pool, PAGE_SIZE, A_HEADS, A_V)),
        'page_table': page_table,
        'state_win0': wins[0],
        'state_win1': wins[1],
        'state_win2': wins[2],
        'w_in': nrm(ks[8], (DEPTH, D_MODEL, IN_TOTAL), D_MODEL ** -0.5),
        'lambda_q1': nrm(ks[9], (DEPTH, HEAD_DIM), 0.1),
        'lambda_k1': nrm(ks[10], (DEPTH, HEAD_DIM), 0.1),
        'lambda_q2': nrm(ks[11], (DEPTH, HEAD_DIM), 0.1),
        'lambda_k2': nrm(ks[12], (DEPTH, HEAD_DIM), 0.1),
        'subln_w': gain(ks[13], A_V),
        'w_b_up': nrm(ks[14], (DEPTH, B_WIDTH, D_MODEL), B_WIDTH ** -0.5),
        'w_out': nrm(ks[15], (DEPTH, D_MODEL, D_MODEL), D_MODEL ** -0.5),
        'mix_pre_norm': gain(ks[16], D_MODEL),
        'mix_post_norm': gain(ks[17], D_MODEL),
        'w_gu': nrm(ks[18], (DEPTH, D_MODEL, 2 * FFN_HIDDEN), D_MODEL ** -0.5),
        'w_down': nrm(ks[19], (DEPTH, FFN_HIDDEN, D_MODEL), FFN_HIDDEN ** -0.5),
        'ffn_pre_norm': gain(ks[20], D_MODEL),
        'ffn_post_norm': gain(ks[21], D_MODEL),
    }

def reference(x_prompt, x_sample, cache_k, cache_v, page_table, state_win0, state_win1, state_win2,
              w_in, lambda_q1, lambda_k1, lambda_q2, lambda_k2, subln_w, w_b_up, w_out,
              mix_pre_norm, mix_post_norm, w_gu, w_down, ffn_pre_norm, ffn_post_norm):
    f32 = jnp.float32
    s_len = x_prompt.shape[1]
    n_dec, t_len = x_sample.shape[:2]
    past_len = page_table.shape[1] * cache_k.shape[2]
    pos_p = jnp.arange(s_len)
    pos_s = past_len + jnp.arange(t_len)
    state_wins = (state_win0, state_win1, state_win2)
    kp_l, vp_l, ks_l, vs_l = [], [], [], []
    winp_l = [[] for _ in DIL_PATTERNS]
    wins_l = [[] for _ in DIL_PATTERNS]
    xp, xs = x_prompt, x_sample
    for l in range(DEPTH):
        lam_init = 0.8 - 0.6 * math.exp(-0.3 * l)
        lam = (jnp.exp(jnp.sum(lambda_q1[l].astype(f32) * lambda_k1[l].astype(f32)))
               - jnp.exp(jnp.sum(lambda_q2[l].astype(f32) * lambda_k2[l].astype(f32))) + lam_init)

        qa, ka, va, qb, kb, vb, ga, gb = project(rmsnorm(xp, mix_pre_norm[l]), w_in[l], pos_p)
        oa = diff_finish(diff_attn_prompt(qa, ka, va, lam), subln_w[l], lam_init, xp.dtype)
        outs, lses = [], []
        for g, (win, dil) in enumerate(DIL_PATTERNS):
            o, lse = dilated_attn_prompt(qb[:, :, g], kb[:, :, g], vb[:, :, g], dil)
            outs.append(o)
            lses.append(lse)
            keep = min(win, s_len)
            winp_l[g].append(jnp.stack([kb[:, s_len - keep:, g], vb[:, s_len - keep:, g]], axis=2))
        xp = merge_branches(xp, oa, combine_groups(outs, lses), ga, gb, w_b_up[l], w_out[l], mix_post_norm[l])
        xp = swiglu_ffn(xp, ffn_pre_norm[l], w_gu[l], w_down[l], ffn_post_norm[l])
        kp_l.append(ka.reshape(ka.shape[0], s_len, A_HEADS, A_QK))
        vp_l.append(va)

        qa, ka, va, qb, kb, vb, ga, gb = project(rmsnorm(xs, mix_pre_norm[l]), w_in[l], pos_s)
        k_past = cache_k[l, page_table].reshape(n_dec, past_len, A_HEADS, 2, HEAD_DIM)
        v_past = cache_v[l, page_table].reshape(n_dec, past_len, A_HEADS, A_V)
        oa = diff_finish(diff_attn_sample(qa, ka, va, k_past, v_past, lam), subln_w[l], lam_init, xs.dtype)
        outs, lses = [], []
        for g, (_, dil) in enumerate(DIL_PATTERNS):
            o, lse, new_buf = dilated_attn_sample(qb[:, :, g], kb[:, :, g], vb[:, :, g], state_wins[g][l], dil)
            outs.append(o)
            lses.append(lse)
            wins_l[g].append(new_buf)
        xs = merge_branches(xs, oa, combine_groups(outs, lses), ga, gb, w_b_up[l], w_out[l], mix_post_norm[l])
        xs = swiglu_ffn(xs, ffn_pre_norm[l], w_gu[l], w_down[l], ffn_post_norm[l])
        ks_l.append(ka.reshape(n_dec, t_len, A_HEADS, A_QK))
        vs_l.append(va)

    return (xp, xs, jnp.stack(kp_l), jnp.stack(vp_l), jnp.stack(ks_l), jnp.stack(vs_l),
            jnp.stack(winp_l[0]), jnp.stack(winp_l[1]), jnp.stack(winp_l[2]),
            jnp.stack(wins_l[0]), jnp.stack(wins_l[1]), jnp.stack(wins_l[2]))


_drawn_inputs = setup_inputs


def setup_inputs(seed=0):
    import zlib

    import numpy as np

    out = dict(_drawn_inputs(seed))
    spreads = {}
    factors = {'lambda_q1': 4.431, 'lambda_k1': 8.0, 'lambda_q2': 8.0, 'lambda_k2': 8.0}
    for name, (base, spread) in spreads.items():
        noise = np.random.default_rng([zlib.crc32(name.encode()), seed]).standard_normal(out[name].shape)
        drawn = base * np.exp(spread * noise) if base else spread * noise
        out[name] = __import__('jax').numpy.asarray(drawn.astype(out[name].dtype))
    for name, factor in factors.items():
        out[name] = (out[name] * factor).astype(out[name].dtype)
    return out
```

```python
import math
from contextlib import ExitStack

import numpy as np
import concourse.bass as bass
from concourse import mybir

ALU = mybir.AluOpType
ACT = mybir.ActivationFunctionType
AX = mybir.AxisListType
F32 = mybir.dt.float32
F32R = mybir.dt.float32r
BF16 = mybir.dt.bfloat16
I32 = mybir.dt.int32
ds = bass.ds

P = 128
D = 1024
KT = D // P
SEQ = 1024
DEC_B, DEC_T = 8, 8
NS = DEC_B * DEC_T
NT = SEQ // P
NTOK = SEQ + NS
PAST = 4096
PAGE = 128
PAGES = PAST // PAGE
E = 64
AH = 8
BH = 4
BW = BH * E
WIN = (128, 512, 2048)
DIL = (1, 4, 16)
ROT = E // 4
HALF = ROT // 2
FFN = -(-(8 * D) // (3 * 256)) * 256
FB = FFN // P
EPS = 1e-6
SCALE = E ** -0.5
LAM_INIT = 0.8 - 0.6 * math.exp(-0.3 * 0)
THETA = 500000.0
NEG = -1.0e30
CH = 512

ZR_QA, ZR_KA, ZR_QB, ZR_KB = 0, D, 2 * D, 2 * D + 3 * BW
ZR = 2 * D + 6 * BW
ZV_A, ZV_B = 0, D
ZV = D + 3 * BW
ZG = 2 * D


def rows_of(t):
    return NS if isinstance(t, int) and t == NT else P


def build(nc, d):
    top = ExitStack()
    with top:
        def sb(ctx, name, shape, dt=F32):
            return ctx.enter_context(nc.sbuf_tensor(name, shape, dt))

        def ps(ctx, name, shape, dt=F32):
            return ctx.enter_context(nc.psum_tensor(name, shape, dt))

        def sem(name):
            return nc.alloc_semaphore(name)

        s_wins = sem("s_wins_copied")
        s_outs = sem("s_outs_copied")
        scratch = {}
        for name, shape in (("zr", [NTOK, ZR]), ("zv", [NTOK, ZV]), ("zg", [NTOK, ZG]),
                            ("oa", [NTOK, D]), ("ob", [NTOK, BW]), ("x1", [NTOK, D])):
            scratch[name] = nc.dram_tensor("scratch_" + name, shape, F32, kind="Internal").ap()
        h2t = [nc.dram_tensor("scratch_h2t_" + part, [P, KT, NTOK], F32, kind="Internal").ap() for part in ("hi", "lo")]
        zr, zv, zg, oa, ob, x1d = (scratch[k] for k in ("zr", "zv", "zg", "oa", "ob", "x1"))

        ident = sb(top, "ident_sb", [P, P])
        identb = sb(top, "identb_sb", [P, P], BF16)
        s_const = sem("s_const")
        eps = sb(top, "eps", [P, 1])
        with nc.cleanup_on_exit():
            norm_in_and_project(nc, d, top, sb, ps, sem, ident, identb, eps, s_const, s_wins, zr, zv, zg)
        lamv = sb(top, "lam_neg", [P, 1])
        with nc.cleanup_on_exit():
            prompt_b(nc, d, sb, ps, sem, ident, identb, zr, zv, ob)
        s_win = [sem(f"db_win{c}") for c in range(len(DB_CHUNKS))]
        windows = ExitStack()
        with windows:
            win = [sb(windows, f"db_win{c}", [P, DB_BATCH, n, 2 * BW]) for c, (_, _, n) in enumerate(DB_CHUNKS)]
            with nc.cleanup_on_exit():
                prompt_a(nc, d, sb, ps, sem, ident, identb, lamv, zr, zv, oa,
                         lambda pool, pace: copy_outputs(pool, pace, d, s_outs, zr, zv),
                         lambda sp, n: load_window(sp, d, win, s_win, 0, *divmod(n, DB_BATCH)))
            with nc.cleanup_on_exit():
                decode_b(nc, d, sb, ps, sem, ident, zr, zv, ob, win, s_win)
        with nc.cleanup_on_exit():
            decode_a(nc, d, sb, ps, sem, ident, lamv, zr, zv, oa)
        with nc.cleanup_on_exit():
            merge(nc, d, sb, ps, sem, ident, eps, oa, ob, zg, x1d, h2t)
        with nc.cleanup_on_exit():
            ffn(nc, d, sb, ps, sem, eps, x1d, h2t)

        with nc.Block() as block:
            @block.sync
            def _(sp):
                sp.wait_ge(s_wins, 16 * DEC_B * len(WIN))
                sp.wait_ge(s_outs, 16 * (2 * NT + 2 + 4 * len(WIN)))


def copy_outputs(pool, pace, d, s_outs, zr, zv):
    for i in range(NT):
        pace(i)
        rows = slice(i * P, (i + 1) * P)
        pool.dma_start(d["new_k_prompt"][rows, :], zr[rows, ZR_KA:ZR_KA + D]).then_inc(s_outs, 16)
        pool.dma_start(d["new_v_prompt"][rows, :], zv[rows, ZV_A:ZV_A + D]).then_inc(s_outs, 16)
    pool.dma_start(d["new_k_sample"], zr[SEQ:NTOK, ZR_KA:ZR_KA + D]).then_inc(s_outs, 16)
    pool.dma_start(d["new_v_sample"], zv[SEQ:NTOK, ZV_A:ZV_A + D]).then_inc(s_outs, 16)
    for g, w in enumerate(WIN):
        keep, past = min(w, SEQ), min(w, PAST)
        for j, (z, col) in enumerate(((zr, ZR_KB), (zv, ZV_B))):
            pace(NT + 2 * g + j)
            cols = slice(col + g * BW, col + (g + 1) * BW)
            pool.dma_start(d[f"new_win{g}_prompt"][:, j, :], z[SEQ - keep:SEQ, cols]).then_inc(s_outs, 16)
            pool.dma_start(d[f"new_win{g}_sample"][:, past - DEC_T:past, j, :],
                           z[SEQ:NTOK, cols].rearrange("(s t) n -> s t n", t=DEC_T)).then_inc(s_outs, 16)


def x_rows(d, t):
    if isinstance(t, int) and t == NT:
        return d["x_sample"]
    return d["x_prompt"][ds(t * P, P), :]


def norm_in_and_project(nc, d, top, sb, ps, sem, ident, identb, eps, s_const, s_wins, zr, zv, zg):
    ctx = ExitStack()
    with ctx:
        hT_hi = sb(ctx, "hT_hi", [P, KT, NTOK], F32R)
        hT_lo = sb(ctx, "hT_lo", [P, KT, NTOK], F32R)
        rope_c = sb(ctx, "rope_c", [P, NT + 1, ROT])
        rope_s = sb(ctx, "rope_s", [P, NT + 1, ROT])
        w_raw = [sb(ctx, f"w_raw{u}", [P, KT, CH]) for u in range(2)]
        w_hi = [sb(ctx, f"w_hi{u}", [P, KT, CH], F32R) for u in range(2)]
        w_lo = [sb(ctx, f"w_lo{u}", [P, KT, CH], F32R) for u in range(2)]
        s_w = [sem(f"s_w{u}") for u in range(2)]
        s_whi = sem("s_whi")
        s_wlo = sem("s_wlo")

        norm = ExitStack()
        with norm:
            gain = sb(norm, "gain_in", [P, D])
            x_sb = [sb(norm, f"x_sb{u}", [P, D]) for u in range(2)]
            h_sb = [sb(norm, f"h_sb{u}", [P, D]) for u in range(2)]
            sq = sb(norm, "sq_in", [P, D])
            ms = [sb(norm, f"ms_in{u}", [P, 2]) for u in range(2)]
            hT_ps = [[ps(norm, f"hT_ps{u}{b}", [P, 4, P]) for b in range(2)] for u in range(2)]
            s_gain = sem("s_gain")
            s_x = [sem(f"s_x{u}") for u in range(2)]
            s_msq = sem("s_msq")
            s_sq = sem("s_sq")
            s_rstd = sem("s_rstd")
            s_h = sem("s_h")
            s_hT = sem("s_hT")
            s_hi = sem("s_hi")
            s_lo = sem("s_lo")
            s_ms = sem("s_ms")
            s_eps = sem("s_eps")
            block = norm.enter_context(nc.Block())

            @block.sync
            def _(sp):
                sp.dma_start(ident[:, :], d["c_ident"]).then_inc(s_const, 16)
                sp.dma_start(identb[:, :], d["c_identb"]).then_inc(s_const, 16)
                sp.dma_start(gain[:, :], d["mix_pre_norm"].to_broadcast([P, D])).then_inc(s_gain, 16)
                sp.dma_start(rope_c[:, :, :], d["c_rope_c"]).then_inc(s_const, 16)
                sp.dma_start(rope_s[:, :, :], d["c_rope_s"]).then_inc(s_const, 16)

                def load(t, u, fresh):
                    if not fresh:
                        sp.wait_ge(s_h, t - 1)
                    r = rows_of(t)
                    sp.dma_start(x_sb[u][0:r, :], x_rows(d, t)).then_inc(s_x[u], 16)

                for u in range(2):
                    load(u, u, True)
                with sp.Fori(1, NT // 2) as i:
                    for u in range(2):
                        load(i * 2 + u, u, False)
                load(NT, 0, False)
                sp.dma_start(w_raw[0][:, :, :], d["w_in"][0, :, :, :]).then_inc(s_w[0], 16)

            def each_tile(eng, step):
                for u in range(2):
                    step(u, u, True)
                with eng.Fori(1, NT // 2) as i:
                    for u in range(2):
                        step(i * 2 + u, u, False)
                step(NT, 0, False)

            @block.gpsimd
            def _(pool):
                nc.gpsimd.memset(eps[:, :], EPS).then_inc(s_eps, 1)

            @block.scalar
            def _(act):
                act.wait_ge(s_eps, 1)

                def mean_square(t, u):
                    r = rows_of(t)
                    act.wait_ge(s_x[u], (t - u) * 8 + 16)
                    if not isinstance(t, int) or t >= 2:
                        act.wait_ge(s_rstd, t - 1)
                    nc.scalar.activation(sq[0:r, :], x_sb[u][0:r, :], ACT.Square,
                                         scale=D ** -0.5, accum_out=ms[u][0:r, 0:1]).then_inc(s_msq, 1)
                    act.wait_ge(s_msq, t + 1)
                    nc.scalar.activation(ms[u][0:r, 0:1], ms[u][0:r, 0:1], ACT.Sqrt, bias=eps[0:r, :])\
                      .then_inc(s_sq, 1)

                def step(t, u, first):
                    r = rows_of(t)
                    if not isinstance(t, int) or t < NT:
                        mean_square(t + 1, 1 - u)
                    act.wait_ge(s_hT, t + 1)
                    for b in range(2):
                        col = ds(t * P, r)
                        nc.scalar.activation(hT_hi[:, 4 * b:4 * b + 4, col], hT_ps[u][b][:, :, 0:r],
                                             ACT.Copy).then_inc(s_hi, 1)
                mean_square(0, 0)
                each_tile(act, step)
                act.wait_ge(s_w[0], 16)
                nc.scalar.activation(w_hi[0][:, :, :], w_raw[0][:, :, :], ACT.Copy).then_inc(s_whi, 1)

            @block.vector
            def _(dve):
                dve.wait_ge(s_gain, 16)

                def normalise(t, u):
                    r = rows_of(t)
                    dve.wait_ge(s_sq, t + 1)
                    nc.vector.reciprocal(ms[u][0:r, 1:2], ms[u][0:r, 0:1]).then_inc(s_ms, 1)
                    dve.wait_ge(s_ms, t + 1)
                    if not isinstance(t, int) or t >= 2:
                        dve.wait_ge(s_hT, t - 1)
                    nc.vector.scalar_tensor_tensor(h_sb[u][0:r, :], x_sb[u][0:r, :], ms[u][0:r, 1:2],
                                                   gain[0:r, :], ALU.mult, ALU.mult).then_inc(s_h, 1)
                    dve.wait_ge(s_h, t + 1)
                    dve.sem_inc(s_rstd, 1)

                def step(t, u, first):
                    r = rows_of(t)
                    if not isinstance(t, int) or t < NT:
                        normalise(t + 1, 1 - u)
                    for b in range(2):
                        col = ds(t * P, r)
                        dve.wait_ge(s_hi, t * 2 + b + 1)
                        nc.vector.tensor_tensor(hT_lo[:, 4 * b:4 * b + 4, col], hT_ps[u][b][:, :, 0:r],
                                                hT_hi[:, 4 * b:4 * b + 4, col].bitcast(F32),
                                                ALU.subtract).then_inc(s_lo, 1)
                normalise(0, 0)
                each_tile(dve, step)
                dve.wait_ge(s_whi, 1)
                nc.vector.tensor_tensor(w_lo[0][:, :, :], w_raw[0][:, :, :], w_hi[0][:, :, :].bitcast(F32),
                                        ALU.subtract).then_inc(s_wlo, 1)

            @block.tensor
            def _(pe):
                pe.wait_ge(s_const, 64)

                def step(t, u, first):
                    r = rows_of(t)
                    pe.wait_ge(s_h, t + 1)
                    if not first:
                        pe.wait_ge(s_lo, t * 2 - 2)
                    for k in range(KT):
                        mm = nc.tensor.transpose(hT_ps[u][k // 4][:, k % 4, 0:r], h_sb[u][0:r, k * P:(k + 1) * P],
                                                 ident[0:r, 0:r])
                    mm.then_inc(s_hT, 1)
                each_tile(pe, step)

        ST = 3
        TILES = NT + 1
        stage = [sb(ctx, f"z_stage{s}", [P, CH]) for s in range(ST)]
        rot_c = sb(ctx, "rot_c", [P, CH // E, ROT])
        rot_s = sb(ctx, "rot_s", [P, CH // E, ROT])
        z_ps = [ps(ctx, f"z_ps{s}", [P, CH]) for s in range(ST)]
        s_z = sem("s_z")
        s_copied = sem("s_copied")
        s_rotp = sem("s_rotp")
        s_staged = sem("s_staged")
        s_stored = [sem(f"s_stored{s}") for s in range(ST)]

        N_ROPE, N_GATE = 6, 4
        tail = [("rope", zr, N_ROPE * CH, CH)] + [("copy", zv, c * CH, min(CH, ZV - c * CH)) for c in range(4)]
        N_CH = N_ROPE + N_GATE + len(tail)

        def each_chunk(eng, step):
            with eng.Fori(0, N_ROPE // 2) as i:
                for u in range(2):
                    step(i * 2 + u, u, "rope", zr, (i * 2 + u) * CH, CH, i * 2 + u)
            with eng.Fori(0, N_GATE // 2) as i:
                for u in range(2):
                    step(i * 2 + u + N_ROPE, u, "gate", zg, (i * 2 + u) * CH, CH, N_ROPE)
            n_rot = N_ROPE
            for j, (kind, dram, col, w) in enumerate(tail):
                c = N_ROPE + N_GATE + j
                step(c, c % 2, kind, dram, col, w, n_rot)
                n_rot += kind == "rope"

        def last(c):
            return isinstance(c, int) and c == N_CH - 1

        block = ctx.enter_context(nc.Block())

        @block.sync
        def _(sp):
            for s in range(ST):
                sp.sem_inc(s_stored[s], 16)

            def load(c, u):
                sp.dma_start(w_raw[u][:, :, :], d["w_in"][ds(c, 1), :, :, :].rearrange("a p k n -> p (a k) n"))\
                  .then_inc(s_w[u], 16)

            def step(c, u, kind, dram, col, w, n_rot):
                if not last(c):
                    sp.wait_ge(s_wlo, c + 1)
                    load(c + 1, 1 - u)
                for t in range(TILES):
                    r = rows_of(t)
                    sp.wait_ge(s_staged, c * TILES + t + 1 + ST)
                    sp.dma_start(dram[t * P:t * P + r, ds(col, w)], stage[t % ST][0:r, 0:w])\
                      .then_inc(s_stored[t % ST], 16)
            each_chunk(sp, step)
            for s in range(ST):
                sp.wait_ge(s_stored[s], 16 + 16 * (TILES // ST) * N_CH)

        @block.scalar
        def _(act):
            act.sem_inc(s_staged, ST)

            def split(c, u):
                act.wait_ge(s_w[u], (c - u) * 8 + 16)
                nc.scalar.activation(w_hi[u][:, :, :], w_raw[u][:, :, :], ACT.Copy).then_inc(s_whi, 1)

            def step(c, u, kind, dram, col, w, n_rot):
                for t in range(TILES):
                    r = rows_of(t)
                    n = c * TILES + t
                    act.wait_ge(s_z, n + 1)
                    if t == 1 and not last(c):
                        split(c + 1, 1 - u)
                    act.wait_ge(s_stored[t % ST], c * 48 + 16 * (t // ST) + 16)
                    if kind == "rope":
                        nc.scalar.activation(stage[t % ST][0:r, :], z_ps[t % ST][0:r, :], ACT.Copy)\
                          .then_inc(s_copied, 1)
                    else:
                        act.wait_ge(s_staged, n + ST)
                        nc.scalar.activation(stage[t % ST][0:r, 0:w], z_ps[t % ST][0:r, 0:w],
                                             ACT.Sigmoid if kind == "gate" else ACT.Copy).then_inc(s_staged, 1)
            each_chunk(act, step)

        @block.vector
        def _(dve):
            def split(c, u):
                dve.wait_ge(s_whi, c + 1)
                nc.vector.tensor_tensor(w_lo[u][:, :, :], w_raw[u][:, :, :], w_hi[u][:, :, :].bitcast(F32),
                                        ALU.subtract).then_inc(s_wlo, 1)

            def step(c, u, kind, dram, col, w, n_rot):
                if kind != "rope":
                    if not last(c):
                        dve.wait_ge(s_z, c * TILES + 2)
                        split(c + 1, 1 - u)
                    return
                for t in range(TILES):
                    r = rows_of(t)
                    m = n_rot * TILES + t
                    dve.wait_ge(s_copied, m + 1)
                    if t == 1 and not last(c):
                        split(c + 1, 1 - u)
                    x = stage[t % ST][0:r, :].rearrange("p (c e) -> p c e", e=E)
                    cos = rope_c[0:r, t:t + 1, :].broadcast_to([r, CH // E, ROT])
                    sin = rope_s[0:r, t:t + 1, :].broadcast_to([r, CH // E, ROT])
                    dve.wait_ge(s_staged, c * TILES + t + ST)
                    nc.vector.tensor_tensor(rot_c[0:r, :, :], x[:, :, 0:ROT], cos, ALU.mult)
                    nc.vector.tensor_tensor(rot_s[0:r, :, 0:HALF], x[:, :, HALF:ROT], sin[:, :, 0:HALF], ALU.mult)
                    nc.vector.tensor_tensor(rot_s[0:r, :, HALF:ROT], x[:, :, 0:HALF], sin[:, :, HALF:ROT],
                                            ALU.mult).then_inc(s_rotp, 1)
                    dve.wait_ge(s_rotp, m + 1)
                    nc.vector.tensor_tensor(x[:, :, 0:ROT], rot_c[0:r, :, :], rot_s[0:r, :, :],
                                            ALU.add).then_inc(s_staged, 1)
            each_chunk(dve, step)

        @block.tensor
        def _(pe):
            def step(c, u, kind, dram, col, w, n_rot):
                pe.wait_ge(s_wlo, c + 1)
                for t in range(TILES):
                    r = rows_of(t)
                    pe.wait_ge(s_staged, c * TILES + t + 1)
                    for k in range(KT):
                        tok = slice(t * P, t * P + r)
                        for a, b in ((hT_hi, w_hi), (hT_lo, w_hi), (hT_hi, w_lo)):
                            mm = nc.tensor.matmul(z_ps[t % ST][0:r, 0:w], a[:, k, tok], b[u][:, k, 0:w],
                                                  start=(k == 0 and a is hT_hi and b is w_hi),
                                                  stop=(k == KT - 1 and b is w_lo))
                    mm.then_inc(s_z, 1)
            each_chunk(pe, step)

        @block.gpsimd
        def _(pool):
            with pool.Fori(0, DEC_B) as s:
                pool.wait_ge(s_staged, s * TILES + 1 + ST)
                for g, w in enumerate(WIN):
                    past = min(w, PAST)
                    rows = "a w c n -> a (w c n)"
                    pool.dma_start(d[f"new_win{g}_sample"][ds(s, 1), 0:past - DEC_T, :, :].rearrange(rows),
                                   d[f"state_win{g}"][ds(s, 1), DEC_T:past, :, :].rearrange(rows)).then_inc(s_wins, 16)


def prompt_a(nc, d, sb, ps, sem, ident, identb, lam_neg, zr, zv, oa, copy_outputs, prefetch):
    ctx = ExitStack()
    with ctx:
        q_in, k_in, v_in = ([sb(ctx, f"pa_{n}{u}", [P, NT, P]) for u in range(2)] for n in "qkv")
        qz = [[sb(ctx, f"pa_qz{u}{c}", [P, SEQ]) for c in range(2)] for u in range(2)]
        kT = [sb(ctx, f"pa_kT{u}", [P, SEQ]) for u in range(2)]
        cmask = sb(ctx, "pa_mask", [P, P], BF16)
        prob = [[sb(ctx, f"pa_prob{u}{c}", [P, SEQ]) for c in range(2)] for u in range(4)]
        aT = [sb(ctx, f"pa_aT{u}", [P, 4, P]) for u in range(2)]
        o_sb = [sb(ctx, f"pa_o{u}", [P, P]) for u in range(2)]
        MAX, BIAS, DEN, REC, FAC = 0, 2, 4, 6, 8
        st = [sb(ctx, f"pa_st{u}", [P, 9]) for u in range(4)]
        s_ps = [ps(ctx, f"pa_s{c}", [P, SEQ]) for c in range(2)]
        t_ps = [ps(ctx, f"pa_t{u}", [P, 4, P]) for u in range(2)]
        o_ps = ps(ctx, "pa_ops", [P, P])
        x_ps = ps(ctx, "pa_x", [P, 4, P])

        lq = sb(ctx, "lam_q", [P, 2, E])
        lk = sb(ctx, "lam_k", [P, 2, E])
        prod = sb(ctx, "lam_prod", [P, 2, E])
        dot = sb(ctx, "lam_dot", [P, 2])
        s_lam_in = sem("s_lam_in")
        s_lam = sem("s_lam_step")
        s_lam_exp = sem("s_lam_exp")
        s_mask = sem("pa_mask_in")
        s_zero = sem("pa_zeroed")
        s_in = [sem(f"pa_in{u}") for u in range(2)]
        s_qk = sem("pa_qk")
        s_qkc = sem("pa_qkc")
        s_s = sem("pa_scored")
        s_bias = sem("pa_bias")
        s_p = sem("pa_prob")
        s_step = sem("pa_step")
        s_a = sem("pa_comb")
        s_t = sem("pa_turned")
        s_tc = sem("pa_turnc")
        s_pv = sem("pa_pv")
        s_o = sem("pa_out")
        s_oc = sem("pa_outc")
        s_st = [sem(f"pa_stored{u}") for u in range(2)]

        groups = [-(-(i + 1) // 4) for i in range(NT)]
        G = sum(groups)
        SMALL = 4

        def bank(i):
            return i % 2 * 512 if i < SMALL else 0
        gbase = [sum(groups[:i]) for i in range(NT)]
        block = ctx.enter_context(nc.Block())

        def heads(step, eng):
            for i in range(NT):
                step(0, 0, i, True)
            with eng.Fori(0, AH // 2 - 1) as j:
                for x in range(2):
                    for i in range(NT):
                        step(j * 2 + 1 + x, 1 - x, i, True)
            for i in range(NT + 2):
                step(AH - 1, 1, i, False)

        def back(h, u, i, n):
            if i - n >= 0:
                return (h, u, i - n) if i - n < NT else None
            return None if isinstance(h, int) and h == 0 else (h - 1, 1 - u, i - n + NT)

        NEXT = 4

        @block.sync
        def _(sp):
            for j in range(2):
                sp.dma_start(lq[:, j, :], d[f"lambda_q{j + 1}"].to_broadcast([P, E])).then_inc(s_lam_in, 16)
                sp.dma_start(lk[:, j, :], d[f"lambda_k{j + 1}"].to_broadcast([P, E])).then_inc(s_lam_in, 16)
            sp.dma_start(cmask[:, :], d["c_causal"]).then_inc(s_mask, 16)
            for u in range(2):
                sp.sem_inc(s_st[u], 16)

            def load(h, u):
                for dst, src, col in ((q_in, zr, ZR_QA), (k_in, zr, ZR_KA), (v_in, zv, ZV_A)):
                    sp.dma_start(dst[u][:, :, :], src[0:SEQ, ds(h * P + col, P)]
                                 .rearrange("(t p) e -> p t e", p=P)).then_inc(s_in[u], 16)

            def step(h, u, final=False):
                if not final:
                    sp.wait_ge(s_o, h * NT + 1)
                    load(h + 1, 1 - u)
                for i in range(NT):
                    sp.wait_ge(s_oc, h * NT + i + 2)
                    sp.dma_start(oa[i * P:(i + 1) * P, ds(h * P, P)], o_sb[i % 2][:, :]).then_inc(s_st[i % 2], 16)
                    if isinstance(h, int):
                        prefetch(sp, (h - AH + 2) * NT + i)
            load(0, 0)
            with sp.Fori(0, AH // 2 - 1) as j:
                for u in range(2):
                    step(j * 2 + u, u)
            step(AH - 2, 0)
            step(AH - 1, 1, True)
            for u in range(2):
                sp.wait_ge(s_st[u], 16 + 16 * AH * NT // 2)

        def lambda_value(dve):
            dve.wait_ge(s_lam_in, 64)
            nc.vector.tensor_tensor(prod[:, :, :], lq[:, :, :], lk[:, :, :], ALU.mult).then_inc(s_lam, 1)
            dve.wait_ge(s_lam, 1)
            nc.vector.tensor_reduce(dot[:, :], prod[:, :, :], AX.X, ALU.add).then_inc(s_lam, 1)
            dve.wait_ge(s_lam_exp, 1)
            nc.vector.tensor_tensor(lam_neg[:, :], dot[:, 1:2], dot[:, 0:1], ALU.subtract).then_inc(s_lam, 1)
            dve.wait_ge(s_lam, 3)
            nc.vector.tensor_scalar(lam_neg[:, :], lam_neg[:, :], -LAM_INIT, None, ALU.add).then_inc(s_lam, 1)
            dve.wait_ge(s_lam, 4)

        @block.gpsimd
        def _(pool):
            for u in range(2):
                for c in range(2):
                    nc.gpsimd.memset(qz[u][c][E * (1 - c):E * (2 - c), :], 0.0).then_inc(s_zero, 1)
            pool.wait_ge(s_in[0], 48)
            pool.wait_ge(s_in[1], 48)
            copy_outputs(pool, lambda n: pool.wait_ge(s_o, n + 2))

        @block.tensor
        def _(pe):
            pe.wait_ge(s_mask, 16)
            pe.wait_ge(s_zero, 4)

            def turn_qk(h, u, m):
                if m == 0:
                    pe.wait_ge(s_in[u], (h - u) * 24 + 48)
                if m > 0 or not isinstance(h, int) or h > 0:
                    pe.wait_ge(s_qkc, h * 4 + m)
                src = (q_in, k_in)[m // 2][u]
                for b in range(4):
                    mm = nc.tensor.transpose(x_ps[:, b, :], src[:, 4 * (m % 2) + b, :], ident[:, :])
                mm.then_inc(s_qk, 1)

            def score(h, u, i, c):
                last = i - 1 if 0 < i < SMALL else i
                pe.wait_ge(s_p, (h * NT + last) * 2 + c + 1)
                n, o = (i + 1) * P, bank(i)
                for b in range(0, n, 512):
                    w = min(512, n - b)
                    nc.tensor.matmul(s_ps[c][:, o + b:o + b + w], qz[u][c][:, i * P:(i + 1) * P], kT[u][:, b:b + w],
                                     start=True, stop=(b + w < n))
                nc.tensor.matmul(s_ps[c][:, o + i * P:o + n], identb[:, :], cmask[:, :], start=False, stop=True)\
                  .then_inc(s_s, 1)

            def turn(h, i):
                pe.wait_ge(s_a, h * NT + i + 1)
                for g in range(groups[i]):
                    n = h * G + gbase[i] + g
                    pe.wait_ge(s_tc, n + 1)
                    for b in range(min(4, i + 1 - 4 * g)):
                        mm = nc.tensor.transpose(t_ps[(gbase[i] + g) % 2][:, b, :],
                                                 prob[i % 4][0][:, (4 * g + b) * P:(4 * g + b + 1) * P], ident[:, :])
                    mm.then_inc(s_t, 1)

            def times_v(h, i, u):
                pe.wait_ge(s_oc, h * NT + i + 1)
                for g in range(groups[i]):
                    pe.wait_ge(s_tc, h * G + gbase[i] + g + 3)
                    for b in range(min(4, i + 1 - 4 * g)):
                        mm = nc.tensor.matmul(o_ps[:, :], aT[(gbase[i] + g) % 2][:, b, :], v_in[u][:, 4 * g + b, :],
                                              start=(g + b == 0), stop=(4 * g + b == i))
                    mm.then_inc(s_pv, 1)
                pe.wait_ge(s_pv, h * G + gbase[i] + groups[i] + 2)
                pe.sem_inc(s_o, 1)

            def step(h, u, i, more):
                out = back(h, u, i, 2)
                if i == 0:
                    pe.wait_ge(s_qkc, h * 4 + 4)
                if i < NT:
                    score(h, u, i, 0)
                    if i < SMALL:
                        score(h, u, i, 1)
                if out:
                    turn(out[0], out[2])
                if SMALL <= i < NT:
                    score(h, u, i, 1)
                if more and NEXT <= i < NEXT + 4:
                    turn_qk(h + 1, 1 - u, i - NEXT)
                if out:
                    times_v(out[0], out[2], out[1])
            for m in range(4):
                turn_qk(0, 0, m)
            heads(step, pe)

        @block.scalar
        def _(act):
            act.sem_inc(s_p, 2)
            act.sem_inc(s_tc, 2)
            act.wait_ge(s_lam, 2)
            nc.scalar.activation(dot[:, :], dot[:, :], ACT.Exp).then_inc(s_lam_exp, 1)

            def copy_turned(h, u, i):
                for g in range(groups[i]):
                    n = h * G + gbase[i] + g
                    b = min(4, i + 1 - 4 * g)
                    act.wait_ge(s_t, n + 1)
                    act.wait_ge(s_pv, n + 1)
                    slot = (gbase[i] + g) % 2
                    nc.scalar.activation(aT[slot][:, 0:b, :], t_ps[slot][:, 0:b, :], ACT.Copy).then_inc(s_tc, 1)

            def step(h, u, i, more):
                out = back(h, u, i, 2)
                if out:
                    copy_turned(*out)
                for c in range(2 if i < NT else 0):
                    act.wait_ge(s_bias, (h * NT + i) * 2 + c + 1)
                    n = (i + 1) * P
                    nc.scalar.activation(prob[i % 4][c][:, 0:n], s_ps[c][:, bank(i):bank(i) + n], ACT.Exp,
                                         scale=SCALE, bias=st[i % 4][:, BIAS + c:BIAS + c + 1],
                                         accum_out=st[i % 4][:, DEN + c:DEN + c + 1]).then_inc(s_p, 1)
            heads(step, act)

        @block.vector
        def _(dve):
            dve.sem_inc(s_oc, 1)
            dve.sem_inc(s_pv, 2)

            lambda_value(dve)

            def copy_qk(h, u, m):
                dve.wait_ge(s_qk, h * 4 + m + 1)
                cols = slice(512 * (m % 2), 512 * (m % 2) + 512)
                if m < 2:
                    nc.vector.tensor_copy(qz[u][0][0:E, cols], x_ps[0:E, :, :])
                    nc.vector.tensor_copy(qz[u][1][E:P, cols], x_ps[E:P, :, :]).then_inc(s_qkc, 1)
                else:
                    nc.vector.tensor_copy(kT[u][:, cols], x_ps[:, :, :]).then_inc(s_qkc, 1)

            def maximum(h, i, c, steps):
                s, gi = st[i % 4], h * NT + i
                dve.wait_ge(s_s, gi * 2 + c + 1)
                nc.vector.tensor_reduce(s[:, MAX + c:MAX + c + 1], s_ps[c][:, bank(i):bank(i) + (i + 1) * P],
                                        AX.X, ALU.max).then_inc(s_step, 1)
                dve.wait_ge(s_step, steps + 1)
                nc.vector.tensor_scalar(s[:, BIAS + c:BIAS + c + 1], s[:, MAX + c:MAX + c + 1], -SCALE,
                                        None, ALU.mult).then_inc(s_bias, 1)

            def combine(h, u, i, steps):
                s, n = st[i % 4], (i + 1) * P
                dve.wait_ge(s_p, (h * NT + i) * 2 + 4)
                nc.vector.reciprocal(s[:, REC:REC + 2], s[:, DEN:DEN + 2]).then_inc(s_step, 1)
                dve.wait_ge(s_step, steps + 1)
                nc.vector.scalar_tensor_tensor(s[:, FAC:FAC + 1], s[:, REC + 1:REC + 2], s[:, DEN:DEN + 1],
                                               lam_neg[:, :], ALU.mult, ALU.mult).then_inc(s_step, 1)
                dve.wait_ge(s_step, steps + 2)
                nc.vector.scalar_tensor_tensor(prob[i % 4][0][:, 0:n], prob[i % 4][1][:, 0:n],
                                               s[:, FAC:FAC + 1], prob[i % 4][0][:, 0:n],
                                               ALU.mult, ALU.add).then_inc(s_a, 1)

            def output(h, u, i):
                dve.wait_ge(s_o, h * NT + i + 1)
                dve.wait_ge(s_st[i % 2], h * 64 + 16 * (i // 2) + 16)
                nc.vector.tensor_scalar(o_sb[i % 2][:, :], o_ps[:, :], st[i % 4][:, REC:REC + 1], None,
                                        ALU.mult).then_inc(s_oc, 1)

            def step(h, u, i, more):
                gi = h * NT + i
                before, out = back(h, u, i, 1), back(h, u, i, 2)
                steps = gi * 4 - 2 if before or i > NT else 0
                if i < NT:
                    if not isinstance(gi, int) or gi >= 4:
                        dve.wait_ge(s_oc, gi - 2)
                    maximum(h, i, 0, steps)
                    steps += 1
                if before:
                    combine(*before, steps)
                    steps += 2
                if i < NT:
                    maximum(h, i, 1, steps)
                if more and NEXT <= i < NEXT + 4:
                    copy_qk(h + 1, 1 - u, i - NEXT)
                if out:
                    output(*out)
            for m in range(4):
                copy_qk(0, 0, m)
            heads(step, dve)


def prompt_b(nc, d, sb, ps, sem, ident, identb, zr, zv, ob):
    NG = len(DIL)
    reach = [w // P for w in WIN]
    def runs(i, g):
        out, far = [], reach[g]
        if i >= far:
            out.append((g, i - far, 1, 2))
        first = max(0, i - far + 1)
        if i > first:
            out.append((g, first, i - first, 1))
        return out + [(g, i, 1, 0)]
    parts = [[runs(i, 2), runs(i, 1) + runs(i, 0)] for i in range(NT)]
    blocks = [[(g, kt + b) for part in parts[i] for g, kt, n, _ in part for b in range(n)] for i in range(NT)]
    width = [[sum(r[2] for r in part) * P for part in parts[i]] for i in range(NT)]
    groups = [-(-len(b) // 4) for b in blocks]
    G = 2 * sum(groups)
    gbase = [[2 * sum(groups[:i]) + c * groups[i] for c in range(2)] for i in range(NT)]
    first = [[2 * sum(min(2, n) for n in groups[:i]) + c * min(2, groups[i]) for c in range(2)] for i in range(NT)]\
        + [[2 * sum(min(2, n) for n in groups)]]
    rest = [[2 * sum(max(0, n - 2) for n in groups[:i]) + c * max(0, groups[i] - 2) for c in range(2)]
            for i in range(NT)] + [[2 * sum(max(0, n - 2) for n in groups)]]
    UNITS = 2 * NT

    ctx = ExitStack()
    with ctx:
        q_in, k_in = ([sb(ctx, f"pb_{n}{g}", [P, NT, P]) for g in range(NG)] for n in "qk")
        v_in = [sb(ctx, f"pb_v{g}", [P, BH // 2 * NT, P]) for g in range(NG)]
        qz = [[sb(ctx, f"pb_qz{g}{c}", [P, SEQ]) for c in range(2)] for g in range(NG)]
        kT = [sb(ctx, f"pb_kT{g}", [P, SEQ]) for g in range(NG)]
        mask = sb(ctx, "pb_mask", [P, NG, 3, P], BF16)
        prob = [sb(ctx, f"pb_prob{u}", [P, max(map(len, blocks)) * P]) for u in range(2)]
        aT = [sb(ctx, f"pb_aT{u}", [P, 4, P]) for u in range(2)]
        o_sb = [sb(ctx, f"pb_o{u}", [P, P]) for u in range(2)]
        MAX, BIAS, DEN, SUM, REC = 0, 2, 3, 5, 6
        st = [sb(ctx, f"pb_st{u}", [P, 7]) for u in range(2)]
        s_ps = [ps(ctx, f"pb_s{x}", [P, SEQ]) for x in range(2)]
        t_ps = [ps(ctx, f"pb_t{u}", [P, 4, P]) for u in range(2)]
        o_ps = ps(ctx, "pb_ops", [P, P])

        s_mask = sem("pb_mask_in")
        s_zero = sem("pb_zeroed")
        s_in = [sem(f"pb_in{g}") for g in range(NG)]
        s_vin = sem("pb_vin")
        s_qk = sem("pb_qk")
        s_qkc = [sem(f"pb_qkc{c}") for c in range(2)]
        s_s = sem("pb_scored")
        s_step = sem("pb_step")
        s_bias = sem("pb_bias")
        s_p = sem("pb_prob")
        s_rec = sem("pb_rec")
        s_t = sem("pb_turned")
        s_tca = sem("pb_turnca")
        s_tcd = sem("pb_turncd")
        s_pv = sem("pb_pv")
        s_o = sem("pb_out")
        s_oc = sem("pb_outc")
        s_st = [sem(f"pb_stored{u}") for u in range(2)]
        block = ctx.enter_context(nc.Block())

        def turned_to(m, c):
            rows, cols = slice(E * c, E * c + E), slice(512 * (m % 2), 512 * (m % 2) + 512)
            return (qz[m // 4][c] if m % 4 < 2 else kT[m // 4])[rows, cols]

        @block.sync
        def _(sp):
            sp.dma_start(mask[:, :, :, :], d["c_dilated"]).then_inc(s_mask, 16)
            for u in range(2):
                sp.sem_inc(s_st[u], 16)

            def rows_in(h, dst, src, col, g):
                return sp.dma_start(dst, src[0:SEQ, h * P + col + g * BW:(h + 1) * P + col + g * BW]
                                    .rearrange("(t p) e -> p t e", p=P))

            def load(h):
                for g in range(NG):
                    rows_in(h, q_in[g][:, :, :], zr, ZR_QB, g).then_inc(s_in[g], 16)
                    rows_in(h, k_in[g][:, :, :], zr, ZR_KB, g).then_inc(s_in[g], 16)
                for g in range(NG):
                    rows_in(h, v_in[g][:, h * NT:(h + 1) * NT, :], zv, ZV_B, g).then_inc(s_vin, 16)

            def step(h):
                for i in range(NT):
                    sp.wait_ge(s_oc, h * UNITS + 2 * i + 3)
                    sp.dma_start(ob[i * P:(i + 1) * P, ds(h * P, P)], o_sb[i % 2][:, :]).then_inc(s_st[i % 2], 16)
            load(0)
            sp.wait_ge(s_s, 1)
            load(1)
            for h in range(BH // 2):
                step(h)
            for u in range(2):
                sp.wait_ge(s_st[u], 16 + 16 * BH // 2 * NT // 2)

        @block.gpsimd
        def _(pool):
            for g in range(NG):
                for c in range(2):
                    nc.gpsimd.memset(qz[g][c][E * (1 - c):E * (2 - c), :], 0.0).then_inc(s_zero, 1)

        @block.tensor
        def _(pe):
            pe.wait_ge(s_mask, 16)
            pe.wait_ge(s_zero, 2 * NG)

            def turn_qk(h):
                for m in range(4 * NG):
                    if m >= 2:
                        pe.wait_ge(s_qkc[0], h * 4 * NG + m - 1)
                        pe.wait_ge(s_qkc[1], h * 4 * NG + m - 1)
                    if m % 4 == 0:
                        pe.wait_ge(s_in[m // 4], h * 32 + 32)
                    src = (q_in, k_in)[m % 4 // 2][m // 4]
                    for b in range(4):
                        mm = nc.tensor.transpose(t_ps[m % 2][:, b, :], src[:, 4 * (m % 2) + b, :], ident[:, :])
                    mm.then_inc(s_qk, 1)
                pe.wait_ge(s_qkc[0], h * 4 * NG + 4 * NG)
                pe.wait_ge(s_qkc[1], h * 4 * NG + 4 * NG)
                pe.wait_ge(s_vin, h * 48 + 48)

            def score(h, i, c, x):
                n = h * UNITS + 2 * i + c
                pe.wait_ge(s_p, n * 2 + x + 1)
                col = 0
                for g, kt, num, m in parts[i][x]:
                    while num:
                        w = min(num, 4 - col // P % 4)
                        nc.tensor.matmul(s_ps[x][:, col:col + w * P], qz[g][c][:, i * P:(i + 1) * P],
                                         kT[g][:, kt * P:(kt + w) * P], start=True, stop=False)
                        mm = nc.tensor.matmul(s_ps[x][:, col:col + w * P], identb[:, :],
                                              mask[:, g, m:m + 1, :].broadcast_to([P, w, P]), start=False, stop=True)
                        col, kt, num = col + w * P, kt + w, num - w
                mm.then_inc(s_s, 1)

            def step(h):
                turn_qk(h)
                for n in range(UNITS + 1):
                    (i, c), (li, lc) = divmod(n, 2), divmod(n - 1, 2)
                    if n < UNITS:
                        score(h, i, c, 0)
                    if n > 0:
                        turn_times_v(h, li, lc, 0)
                    if n < UNITS:
                        score(h, i, c, 1)
                    if n > 0:
                        turn_times_v(h, li, lc, 1)

            def turn_times_v(h, i, c, half):
                base, all_ = h * G + gbase[i][c], len(blocks[i])

                def copied(g):
                    if g < 2:
                        pe.wait_ge(s_tca, h * first[NT][0] + first[i][c] + g + 1)
                    else:
                        pe.wait_ge(s_tcd, h * rest[NT][0] + rest[i][c] + g - 1)

                def turned(g):
                    if g >= 2:
                        copied(g - 2)
                    for b in range(4 * g, min(4 * g + 4, all_)):
                        mm = nc.tensor.transpose(t_ps[(gbase[i][c] + g) % 2][:, b % 4, :],
                                                 prob[c][:, b * P:(b + 1) * P], ident[:, :])
                    mm.then_inc(s_t, 1)
                if half == 0:
                    pe.wait_ge(s_p, (h * UNITS + 2 * i + c) * 2 + 4)
                    for g in range(min(2, groups[i])):
                        turned(g)
                    return
                pe.wait_ge(s_oc, h * UNITS + 2 * i + c + 1)
                for g in range(groups[i]):
                    copied(g)
                    for b in range(4 * g, min(4 * g + 4, all_)):
                        vg, kt = blocks[i][b]
                        mm = nc.tensor.matmul(o_ps[:, :], aT[(gbase[i][c] + g) % 2][:, b % 4, :], v_in[vg][:, ds(h * NT + kt, 1), :].rearrange("p a e -> p (a e)"),
                                              start=(b == 0), stop=(b == all_ - 1))
                    mm.then_inc(s_pv, 1)
                    if g + 2 < groups[i]:
                        turned(g + 2)
                pe.wait_ge(s_pv, base + groups[i] + 2)
                pe.sem_inc(s_o, 1)
            with pe.Fori(0, BH // 2) as h:
                step(h)

        @block.scalar
        def _(act):
            act.sem_inc(s_p, 2)

            def copy_groups(h, i, c, some):
                for g in some:
                    n = h * G + gbase[i][c] + g
                    b = min(4, len(blocks[i]) - 4 * g)
                    act.wait_ge(s_t, n + 1)
                    act.wait_ge(s_pv, n + 1)
                    slot = (gbase[i][c] + g) % 2
                    nc.scalar.activation(aT[slot][:, 0:b, :], t_ps[slot][:, 0:b, :], ACT.Copy).then_inc(s_tca, 1)

            def step(h):
                for m in range(4 * NG):
                    act.wait_ge(s_qk, h * 4 * NG + m + 1)
                    nc.scalar.activation(turned_to(m, 1), t_ps[m % 2][E:P, :, :].rearrange("p b t -> p (b t)"),
                                         ACT.Copy).then_inc(s_qkc[1], 1)
                for n in range(UNITS + 1):
                    (i, c), (li, lc) = divmod(n, 2), divmod(n - 1, 2)
                    if n > 0:
                        copy_groups(h, li, lc, range(min(2, groups[li])))
                    if n < UNITS:
                        unit = h * UNITS + n
                        act.wait_ge(s_bias, unit + 1)
                        nx, ny = width[i]
                        for x, (a, b) in enumerate(((0, nx), (nx, nx + ny))):
                            nc.scalar.activation(prob[c][:, a:b], s_ps[x][:, 0:b - a], ACT.Exp, scale=SCALE,
                                                 bias=st[c][:, BIAS:BIAS + 1],
                                                 accum_out=st[c][:, DEN + x:DEN + x + 1]).then_inc(s_p, 1)
            with act.Fori(0, BH // 2) as h:
                step(h)

        @block.vector
        def _(dve):
            dve.sem_inc(s_oc, 1)
            dve.sem_inc(s_pv, 2)

            def step(h):
                for m in range(4 * NG):
                    dve.wait_ge(s_qk, h * 4 * NG + m + 1)
                    nc.vector.tensor_copy(turned_to(m, 0), t_ps[m % 2][0:E, :, :]).then_inc(s_qkc[0], 1)
                for n in range(UNITS + 1):
                    i, c = divmod(n, 2)
                    unit = h * UNITS + n
                    s = st[c]
                    if n < UNITS:
                        dve.wait_ge(s_oc, unit)
                        for x in range(2):
                            dve.wait_ge(s_s, unit * 2 + x + 1)
                            nc.vector.tensor_reduce(s[:, MAX + x:MAX + x + 1], s_ps[x][:, 0:width[i][x]], AX.X,
                                                    ALU.max).then_inc(s_step, 1)
                        dve.wait_ge(s_step, unit * 3 + 2)
                        nc.vector.tensor_scalar(s[:, BIAS:BIAS + 1], s[:, MAX:MAX + 1], s[:, MAX + 1:MAX + 2],
                                                -SCALE, ALU.max, ALU.mult).then_inc(s_bias, 1)
                    if n > 0:
                        li, lc = divmod(n - 1, 2)
                        for g in range(2, groups[li]):
                            k = h * G + gbase[li][lc] + g
                            b = min(4, len(blocks[li]) - 4 * g)
                            dve.wait_ge(s_t, k + 1)
                            dve.wait_ge(s_pv, k + 1)
                            slot = (gbase[li][lc] + g) % 2
                            nc.vector.tensor_copy(aT[slot][:, 0:b, :], t_ps[slot][:, 0:b, :]).then_inc(s_tcd, 1)
                        dve.wait_ge(s_o, unit)
                        if lc == 0:
                            dve.wait_ge(s_st[li % 2], h * 64 + 16 * (li // 2) + 16)
                        nc.vector.tensor_scalar(o_sb[li % 2][:, lc * E:lc * E + E], o_ps[:, lc * E:lc * E + E],
                                                st[lc][:, REC:REC + 1], None, ALU.mult).then_inc(s_oc, 1)
                    if n < UNITS:
                        dve.wait_ge(s_p, unit * 2 + 4)
                        nc.vector.tensor_tensor(s[:, SUM:SUM + 1], s[:, DEN:DEN + 1], s[:, DEN + 1:DEN + 2],
                                                ALU.add).then_inc(s_step, 1)
                        dve.wait_ge(s_step, unit * 3 + 3)
                        nc.vector.reciprocal(s[:, REC:REC + 1], s[:, SUM:SUM + 1]).then_inc(s_rec, 1)
                        dve.wait_ge(s_rec, unit + 1)
            with dve.Fori(0, BH // 2) as h:
                step(h)


def decode_a(nc, d, sb, ps, sem, ident, lam_neg, zr, zv, oa):
    NGR, PPG, SLOTS = PAGES // 4, 4, 4
    ORDER = (0, 2, 4, 6, 1, 3, 5, 7)
    W = PPG * PAGE
    ctx = ExitStack()
    with ctx:
        table = sb(ctx, "da_table", [1, DEC_B * PAGES], I32)
        page = [sb(ctx, f"da_page{n}", [P, PPG, D]) for n in range(SLOTS)]
        k_new = sb(ctx, "da_knew", [DEC_T, D])
        v_new = sb(ctx, "da_vnew", [P, D])
        q_in = sb(ctx, "da_q", [NS, D])
        qT = sb(ctx, "da_qT", [P, AH, NS])
        qs = sb(ctx, "da_qs", [P, AH, 32])
        kT = [sb(ctx, f"da_kT{n}", [P, W]) for n in range(8)]
        kTn = sb(ctx, "da_kTn", [P, AH, DEC_T])
        s_sb = sb(ctx, "da_scores", [P, PAST + PAGE])
        nmask = sb(ctx, "da_nmask", [P, DEC_T])
        pT = [sb(ctx, f"da_pT{u}", [P, PPG, P]) for u in range(2)]
        cmax = sb(ctx, "da_cmax", [P, NGR + 1])
        den = sb(ctx, "da_den", [P, NGR + 1])
        MX, BIAS, SUM, REC, CF, FAC = range(6)
        st = sb(ctx, "da_st", [P, 6])
        comp = sb(ctx, "da_comp", [P, 2])
        sel = sb(ctx, "da_sel", [P, 2, NS])
        o_n = sb(ctx, "da_on", [P, 2 * P])
        o_fin = sb(ctx, "da_ofin", [NS, P])
        t_ps = [ps(ctx, f"da_t{n}", [P, PPG, PAGE]) for n in range(4)]
        s_ps = [ps(ctx, f"da_s{n}", [P, W]) for n in range(2)]
        p_ps = ps(ctx, "da_p", [P, PPG, P])
        o_ps = ps(ctx, "da_o", [P, 512])

        s_cst = sem("da_const")
        s_zero = sem("da_zero")
        s_page = [sem(f"da_page{n}") for n in range(SLOTS)]
        s_vused = sem("da_vused")
        s_new = sem("da_new")
        s_newfree = sem("da_newfree")
        s_qt = sem("da_qt")
        s_qtc = sem("da_qtc")
        s_qs = sem("da_qsready")
        s_kt = sem("da_kt")
        s_kca = sem("da_kca")
        s_kcd = sem("da_kcd")
        s_qk = sem("da_qk")
        s_kn = sem("da_kn")
        s_knc = sem("da_knc")
        s_sn = sem("da_sn")
        s_sc = sem("da_sc")
        s_snc = sem("da_snc")
        s_step = sem("da_step")
        s_bias = sem("da_bias")
        s_exp = sem("da_exp")
        s_pt = sem("da_pt")
        s_ptc = sem("da_ptc")
        s_o = sem("da_out")
        s_on = sem("da_on")
        s_f = sem("da_fin")
        s_fc = sem("da_finc")
        s_ofree = sem("da_ofree")
        s_st = sem("da_stored")
        block = ctx.enter_context(nc.Block())

        @block.sync
        def _(sp):
            for dst, name in ((table, "page_table"), (nmask, "c_new_mask"), (comp, "c_comp")):
                sp.dma_start(dst[:, :], d[name]).then_inc(s_cst, 16)
            sp.dma_start(sel[:, :, :], d["c_sel"]).then_inc(s_cst, 16)
            sp.dma_start(q_in[:, :], zr[SEQ:NTOK, ZR_QA:ZR_QA + D]).then_inc(s_cst, 16)
            sp.wait_ge(s_cst, 80)
            with sp.Fori(0, DEC_B) as s:
                for l in range(2 * NGR):
                    cache = d["cache_k"] if l < NGR else d["cache_v"]
                    if l == NGR // 2:
                        sp.wait_ge(s_newfree, s + 1)
                        sp.dma_start(k_new[:, :], zr[ds(s * DEC_T + SEQ, DEC_T), ZR_KA:ZR_KA + D]).then_inc(s_new, 16)
                        sp.dma_start(v_new[0:DEC_T, :], zv[ds(s * DEC_T + SEQ, DEC_T), ZV_A:ZV_A + D])\
                          .then_inc(s_new, 16)
                    pages = [sp.value_load(table[0:1, ds(s * PAGES + (l % NGR) * PPG + j, 1)], min_val=0,
                                           max_val=cache.shape[0] - 1) for j in range(PPG)]
                    if SLOTS <= l < NGR + SLOTS:
                        sp.wait_ge(s_kt, s * 8 * NGR + 8 * (l - SLOTS + 1))
                    else:
                        sp.wait_ge(s_vused, s * NGR + (l + SLOTS if l < SLOTS else l - SLOTS) % NGR + 1
                                   + (NGR if l > SLOTS else 0))
                    for j, pg in enumerate(pages):
                        sp.dma_start(page[l % SLOTS][:, j, :], cache[ds(pg, 1), :, :]
                                     .rearrange("a p n -> p (a n)")).then_inc(s_page[l % SLOTS], 16)

        def page_count(s, l):
            return s * (2 * NGR // SLOTS * 64) + (l // SLOTS + 1) * 64

        @block.gpsimd
        def _(pool):
            nc.gpsimd.memset(v_new[:, :], 0.0).then_inc(s_zero, 1)
            nc.gpsimd.memset(qs[:, :, :], 0.0).then_inc(s_zero, 1)
            nc.gpsimd.memset(s_sb[:, PAST:], 0.0).then_inc(s_zero, 1)
            pool.wait_ge(s_zero, 3)
            pool.sem_inc(s_newfree, 1)
            pool.sem_inc(s_ofree, 1)
            with pool.Fori(0, DEC_B) as s:
                pool.wait_ge(s_fc, s + 1)
                pool.dma_start(oa[ds(s * DEC_T + SEQ, DEC_T), :].rearrange("q (h e) -> h q e", h=AH),
                               o_fin[:, :]).then_inc(s_st, 16)
                pool.wait_ge(s_st, s * 16 + 16)
                pool.sem_inc(s_ofree, 1)

        @block.tensor
        def _(pe):
            pe.sem_inc(s_vused, NGR)
            pe.sem_inc(s_qk, 2)
            pe.wait_ge(s_cst, 80)
            for h in range(AH):
                mm = nc.tensor.transpose(p_ps[:, h // 2, (h % 2) * NS:(h % 2) * NS + NS],
                                         q_in[:, h * P:(h + 1) * P], ident[0:NS, 0:NS])
            mm.then_inc(s_qt, 1)
            pe.wait_ge(s_qtc, 1)
            pe.wait_ge(s_zero, 3)

            def turn_keys(s, g, half):
                if half == 0:
                    pe.wait_ge(s_page[g % SLOTS], page_count(s, g))
                for j in range(4):
                    n = s * 4 * NGR + g * 4 + 2 * half + j // 2 + 1
                    pe.wait_ge(s_kca if j % 2 == 0 else s_kcd, n)
                    h = ORDER[4 * half + j]
                    for b in range(PPG):
                        mm = nc.tensor.transpose(t_ps[j][:, b, :], page[g % SLOTS][:, b, h * P:(h + 1) * P],
                                                 ident[:, :])
                    mm.then_inc(s_kt, 1)

            def score(s, g, half):
                n = s * 4 * NGR + g * 4 + 2 * half + 4
                pe.wait_ge(s_kca, n)
                pe.wait_ge(s_kcd, n)
                if half == 0:
                    pe.wait_ge(s_sc, s * NGR + g + 1)
                for j in range(4):
                    h = ORDER[4 * half + j]
                    mm = nc.tensor.matmul(s_ps[g % 2][32 * j:32 * j + 32, :], qs[:, h, :], kT[4 * half + j][:, :],
                                          start=(half == 0), stop=(half == 1))
                mm.then_inc(s_qk, 1)

            def turn_probs(s, g):
                pe.wait_ge(s_exp, s * (NGR + 1) + g + 1)
                pe.wait_ge(s_ptc, s * (NGR + 1) + g + 1)
                for b in range(PPG if g < NGR else 1):
                    mm = nc.tensor.transpose(p_ps[:, b, :], s_sb[:, g * W + b * PAGE:g * W + (b + 1) * PAGE], ident[:, :])
                mm.then_inc(s_pt, 1)

            def times_v(s, g):
                if g < NGR:
                    pe.wait_ge(s_page[g % SLOTS], page_count(s, NGR + g))
                else:
                    pe.wait_ge(s_new, s * 32 + 32)
                pe.wait_ge(s_ptc, s * (NGR + 1) + g + 2)
                for b in range(PPG if g < NGR else 1):
                    for q in range(4):
                        v = page[g % SLOTS][:, b, q * 256:(q + 1) * 256] if g < NGR else v_new[:, q * 256:(q + 1) * 256]
                        mm = nc.tensor.matmul(o_ps[32 * q:32 * q + 32, 0:256], pT[g % 2][:, b, 32 * q:32 * q + 32], v,
                                              start=(g == 0 and b == 0), stop=(g == NGR))
                mm.then_inc(s_vused if g < NGR else s_o, 1)

            with pe.Fori(0, DEC_B) as s:
                for g in range(NGR):
                    for half in range(2):
                        turn_keys(s, g, half)
                        if g + half > 0:
                            if g == 0:
                                pe.wait_ge(s_qs, s + 1)
                            score(s, *divmod(2 * g + half - 1, 2))
                pe.wait_ge(s_new, s * 32 + 32)
                score(s, NGR - 1, 1)
                for h in range(AH):
                    mm = nc.tensor.transpose(p_ps[:, 0, h * DEC_T:(h + 1) * DEC_T], k_new[:, h * P:(h + 1) * P],
                                             ident[0:DEC_T, 0:DEC_T])
                mm.then_inc(s_kn, 1)
                pe.wait_ge(s_knc, s + 1)
                pe.wait_ge(s_sc, s * NGR + NGR - 1 + 2)
                for h in ORDER:
                    mm = nc.tensor.matmul(s_ps[0][32 * (h // 2):32 * (h // 2) + 32, 0:DEC_T], qs[:, h, :],
                                          kTn[:, h, :], start=(h % 2 == 0), stop=(h % 2 == 1))
                mm.then_inc(s_sn, 1)
                turn_probs(s, 0)
                for g in range(NGR + 1):
                    if g < NGR:
                        turn_probs(s, g + 1)
                    times_v(s, g)
                pe.wait_ge(s_on, s + 1)
                pe.sem_inc(s_newfree, 1)
                for par in range(2):
                    mm = nc.tensor.matmul(o_ps[0:NS, 256:256 + P], sel[:, par, :], o_n[:, par * P:(par + 1) * P],
                                          start=(par == 0), stop=(par == 1))
                mm.then_inc(s_f, 1)

        @block.scalar
        def _(act):
            act.sem_inc(s_kca, 2)
            act.sem_inc(s_sc, 2)
            with act.Fori(0, DEC_B) as s:
                def copy_scores(g):
                    act.wait_ge(s_qk, s * 2 * NGR + 2 * g + 2 + 2)
                    nc.scalar.activation(s_sb[:, g * W:(g + 1) * W], s_ps[g % 2][:, :], ACT.Copy).then_inc(s_sc, 1)
                for g in range(NGR):
                    for half in range(2):
                        act.wait_ge(s_qk, s * 2 * NGR + 2 * g + half + 1)
                        for j in (0, 2):
                            act.wait_ge(s_kt, s * 8 * NGR + 8 * g + 4 * half + j + 1)
                            nc.scalar.activation(kT[4 * half + j][:, :], t_ps[j][:, :, :], ACT.Copy).then_inc(s_kca, 1)
                        if half == 0 and g > 0:
                            copy_scores(g - 1)
                copy_scores(NGR - 1)
                act.wait_ge(s_kn, s + 1)
                nc.scalar.activation(kTn[:, :, :], p_ps[:, 0, 0:AH * DEC_T].rearrange("p (h t) -> p h t", h=AH),
                                     ACT.Copy).then_inc(s_knc, 1)
                act.wait_ge(s_bias, s + 1)
                for g in range(NGR + 1):
                    cols = s_sb[:, g * W:(g + 1) * W] if g < NGR else s_sb[:, PAST:PAST + DEC_T]
                    nc.scalar.activation(cols, cols, ACT.Exp, scale=SCALE, bias=st[:, BIAS:BIAS + 1],
                                         accum_out=den[:, g:g + 1]).then_inc(s_exp, 1)

        @block.vector
        def _(dve):
            dve.sem_inc(s_kcd, 2)
            dve.sem_inc(s_ptc, 1)
            dve.wait_ge(s_cst, 80)
            nc.vector.scalar_tensor_tensor(st[:, CF:CF + 1], comp[:, 1:2], lam_neg[:, :], comp[:, 0:1], ALU.mult,
                                           ALU.add).then_inc(s_step, 1)
            dve.wait_ge(s_qt, 1)
            nc.vector.tensor_copy(qT[:, :, :], p_ps[:, :, :].rearrange("p a (b t) -> p (a b) t", b=2))\
              .then_inc(s_qtc, 1)
            dve.wait_ge(s_zero, 3)
            dve.wait_ge(s_qtc, 1)
            S = 4
            with dve.Fori(0, DEC_B) as s:
                for par in range(2):
                    for c in range(2):
                        rows, col = slice(E * c, E * c + E), par * 16 + c * 8
                        ins = nc.vector.tensor_copy(qs[rows, par::2, col:col + DEC_T],
                                                    qT[rows, par::2, ds(s * DEC_T, DEC_T)])
                ins.then_inc(s_qs, 1)

                def chunk_max(g):
                    dve.wait_ge(s_sc, s * NGR + g + 1 + 2)
                    nc.vector.tensor_reduce(cmax[:, g:g + 1], s_sb[:, g * W:(g + 1) * W], AX.X, ALU.max)
                for g in range(NGR):
                    for half in range(2):
                        dve.wait_ge(s_qk, s * 2 * NGR + 2 * g + half + 1)
                        for j in (1, 3):
                            dve.wait_ge(s_kt, s * 8 * NGR + 8 * g + 4 * half + j + 1)
                            nc.vector.tensor_copy(kT[4 * half + j][:, :], t_ps[j][:, :, :]).then_inc(s_kcd, 1)
                        if half == 1 and g > 0:
                            chunk_max(g - 1)
                chunk_max(NGR - 1)
                dve.wait_ge(s_sn, s + 1)
                new = s_sb[:, PAST:PAST + DEC_T]
                nc.vector.tensor_tensor(new, s_ps[0][:, 0:DEC_T], nmask[:, :], ALU.add).then_inc(s_snc, 1)
                dve.wait_ge(s_snc, s + 1)
                nc.vector.tensor_reduce(cmax[:, NGR:NGR + 1], new, AX.X, ALU.max).then_inc(s_step, 1)
                dve.wait_ge(s_step, s * S + 2)
                nc.vector.tensor_reduce(st[:, MX:MX + 1], cmax[:, :], AX.X, ALU.max).then_inc(s_step, 1)
                dve.wait_ge(s_step, s * S + 3)
                nc.vector.tensor_scalar(st[:, BIAS:BIAS + 1], st[:, MX:MX + 1], -SCALE, None,
                                        ALU.mult).then_inc(s_bias, 1)
                for g in range(NGR + 1):
                    b = PPG if g < NGR else 1
                    dve.wait_ge(s_pt, s * (NGR + 1) + g + 1)
                    nc.vector.tensor_copy(pT[g % 2][:, 0:b, :], p_ps[:, 0:b, :]).then_inc(s_ptc, 1)
                nc.vector.tensor_reduce(st[:, SUM:SUM + 1], den[:, :], AX.X, ALU.add).then_inc(s_step, 1)
                dve.wait_ge(s_step, s * S + 4)
                nc.vector.reciprocal(st[:, REC:REC + 1], st[:, SUM:SUM + 1]).then_inc(s_step, 1)
                dve.wait_ge(s_step, s * S + 5)
                dve.wait_ge(s_o, s + 1)
                nc.vector.tensor_scalar(o_n[:, :], o_ps[:, 0:2 * P], st[:, REC:REC + 1], st[:, CF:CF + 1], ALU.mult,
                                        ALU.mult).then_inc(s_on, 1)
                dve.wait_ge(s_f, s + 1)
                dve.wait_ge(s_ofree, s + 1)
                nc.vector.tensor_copy(o_fin[:, :], o_ps[0:NS, 256:256 + P]).then_inc(s_fc, 1)


DB_BATCH = 4
DB_CHUNKS = [(2, 0, 4), (2, 4, 4), (1, 0, 4), (0, 0, 1)]


def load_window(sp, d, win, s_win, batch, c, s):
    g, t0, n = DB_CHUNKS[c]
    src = d[f"state_win{g}"][batch * DB_BATCH + s, :, :, :].rearrange("(p j) c n -> p j (c n)", p=P)
    sp.dma_start(win[c][:, s, :, :], src[:, t0:t0 + n, :]).then_inc(s_win[c], 16)


def decode_b(nc, d, sb, ps, sem, ident, zr, zv, ob, win, s_win):
    NB = DB_BATCH
    NG = len(DIL)
    tiles = [min(dl, DEC_T) for dl in DIL]
    chunks = DB_CHUNKS
    NC = len(chunks)
    NEW = NG * DEC_T
    COLS = sum(tiles) * P + NEW
    ctx = ExitStack()
    with ctx:
        k_new = sb(ctx, "db_knew", [P, NB, BW])
        v_new = sb(ctx, "db_vnew", [P, NB, BW])
        q_in = sb(ctx, "db_q", [NS, NG * BW])
        qT = sb(ctx, "db_qT", [P, 2, NG, NS])
        qs = sb(ctx, "db_qs", [P, 2, NB, NG, 32])
        kT = [sb(ctx, f"db_kT{n}", [P, 4 * P]) for n in range(8)]
        s_sb = sb(ctx, "db_scores", [P, (sum(tiles) + 1) * P])
        mask = sb(ctx, "db_mask", [P, COLS])
        head = sb(ctx, "db_head", [P, BH])
        pT = [sb(ctx, f"db_pT{u}", [P, 4, P]) for u in range(2)]
        cmax = sb(ctx, "db_cmax", [P, NC])
        den = sb(ctx, "db_den", [P, NC])
        MX, BIAS, SUM, REC = range(4)
        st = sb(ctx, "db_st", [P, 4])
        fac = sb(ctx, "db_fac", [P, BH])
        o_sb = sb(ctx, "db_osb", [P, E])
        t_ps = [ps(ctx, f"db_t{n}", [P, 4, P]) for n in range(4)]
        s_ps = [ps(ctx, f"db_s{n}", [P, 4 * P]) for n in range(2)]
        p_ps = ps(ctx, "db_p", [P, 4, P])
        o_ps = ps(ctx, "db_o", [P, BW])

        s_cst = sem("db_const")
        s_zero = sem("db_zero")
        s_new = sem("db_new")
        s_qt = sem("db_qt")
        s_qtc = sem("db_qtc")
        s_qs = sem("db_qsready")
        s_kt = sem("db_kt")
        s_kca = sem("db_kca")
        s_kcd = sem("db_kcd")
        s_qk = sem("db_qk")
        s_sc = sem("db_sc")
        s_step = sem("db_step")
        s_bias = sem("db_bias")
        s_exp = sem("db_exp")
        s_pt = sem("db_pt")
        s_ptc = sem("db_ptc")
        s_v = sem("db_v")
        s_on = sem("db_on")
        s_acc = sem("db_acc")
        s_free = sem("db_free")
        s_st = sem("db_stored")
        block = ctx.enter_context(nc.Block())
        off = [0]
        for _, _, n in chunks:
            off.append(off[-1] + n * P)
        wide = [n * P for _, _, n in chunks]
        wide[-1] += NEW

        def store(sp, batch):
            sp.wait_ge(s_on, batch + 1)
            for s in range(NB):
                row = SEQ + (batch * NB + s) * DEC_T
                sp.dma_start(ob[row:row + DEC_T, :].rearrange("q (h e) -> h q e", h=BH),
                             o_sb[32 * s:32 * s + 32, :]).then_inc(s_st, 16)
            sp.wait_ge(s_st, (batch + 1) * NB * 16)
            sp.sem_inc(s_free, 1)

        @block.sync
        def _(sp):
            sp.dma_start(mask[:, :], d["c_win_mask"]).then_inc(s_cst, 16)
            sp.dma_start(head[:, :], d["c_head"]).then_inc(s_cst, 16)
            sp.dma_start(q_in[:, :], zr[SEQ:NTOK, ZR_QB:ZR_QB + NG * BW]).then_inc(s_cst, 16)
            sp.wait_ge(s_zero, 4)
            sp.sem_inc(s_free, 1)
            for batch in range(DEC_B // NB):
                for c in range(NC if batch > 0 else 0):
                    sp.wait_ge(s_v, batch * NC + c + 1)
                    for s in range(NB):
                        load_window(sp, d, win, s_win, batch, c, s)
                if batch > 0:
                    sp.wait_ge(s_v, (batch + 1) * NC)
                for s in range(NB):
                    rows = slice(SEQ + (batch * NB + s) * DEC_T, SEQ + (batch * NB + s + 1) * DEC_T)
                    for g in range(NG):
                        for dst, z, col in ((k_new, zr, ZR_KB), (v_new, zv, ZV_B)):
                            sp.dma_start(dst[g * DEC_T:(g + 1) * DEC_T, s, :],
                                         z[rows, col + g * BW:col + (g + 1) * BW]).then_inc(s_new, 16)
                if batch > 0:
                    store(sp, batch - 1)
            store(sp, DEC_B // NB - 1)

        @block.gpsimd
        def _(pool):
            nc.gpsimd.memset(v_new[:, :, :], 0.0).then_inc(s_zero, 1)
            nc.gpsimd.memset(k_new[:, :, :], 0.0).then_inc(s_zero, 1)
            nc.gpsimd.memset(qs[:, :, :, :, :], 0.0).then_inc(s_zero, 1)
            nc.gpsimd.memset(s_sb[:, COLS:], 0.0).then_inc(s_zero, 1)

        @block.tensor
        def _(pe):
            pe.sem_inc(s_v, NC)
            pe.sem_inc(s_qk, 2)
            pe.wait_ge(s_cst, 48)
            for g in range(NG):
                for pair in range(2):
                    n = pair * NG + g
                    mm = nc.tensor.transpose(p_ps[:, n // 2, n % 2 * NS:n % 2 * NS + NS],
                                             q_in[:, g * BW + pair * P:g * BW + (pair + 1) * P], ident[0:NS, 0:NS])
            mm.then_inc(s_qt, 1)
            pe.wait_ge(s_qtc, 1)
            pe.wait_ge(s_zero, 4)

            def turn_keys(bt, c, pair):
                g, t0, n = chunks[c]
                pe.wait_ge(s_win[c], bt * 64 + 64)
                if c == NC - 1:
                    pe.wait_ge(s_new, bt * NB * NG * 32 + NB * NG * 32)
                for s in range(NB):
                    pe.wait_ge(s_kca if s % 2 == 0 else s_kcd, bt * 4 * NC + c * 4 + 2 * pair + s // 2 + 1)
                    for b in range(n):
                        mm = nc.tensor.transpose(t_ps[s][:, b, :], win[c][:, s, b, pair * P:(pair + 1) * P], ident[:, :])
                    if c == NC - 1:
                        mm = nc.tensor.transpose(t_ps[s][:, n, :], k_new[:, s, pair * P:(pair + 1) * P], ident[:, :])
                    mm.then_inc(s_kt, 1)

            def score(bt, c, pair):
                g, t0, n = chunks[c]
                k = bt * 4 * NC + c * 4 + 2 * pair + 4
                pe.wait_ge(s_kca, k)
                pe.wait_ge(s_kcd, k)
                if pair == 0:
                    pe.wait_ge(s_sc, bt * NC + c + 1)
                for s in range(NB):
                    mm = nc.tensor.matmul(s_ps[c % 2][32 * s:32 * s + 32, 0:n * P], qs[:, pair, s, g, :],
                                          kT[4 * pair + s][:, 0:n * P], start=(pair == 0), stop=(pair == 1),
                                          skip_group_check=True)
                if c == NC - 1:
                    for ng in range(NG):
                        a = n * P + ng * DEC_T
                        for s in range(NB):
                            mm = nc.tensor.matmul(s_ps[c % 2][32 * s:32 * s + 32, a:a + DEC_T], qs[:, pair, s, ng, :],
                                                  kT[4 * pair + s][:, a:a + DEC_T], start=False, stop=(pair == 1),
                                                  skip_group_check=True)
                mm.then_inc(s_qk, 1)

            def turn_probs(bt, c):
                pe.wait_ge(s_exp, bt * NC + c + 1)
                pe.wait_ge(s_ptc, bt * NC + c + 1)
                for b in range(chunks[c][2] + (c == NC - 1)):
                    mm = nc.tensor.transpose(p_ps[:, b, :], s_sb[:, off[c] + b * P:off[c] + (b + 1) * P], ident[:, :])
                mm.then_inc(s_pt, 1)

            def times_v(bt, c):
                n = chunks[c][2]
                pe.wait_ge(s_ptc, bt * NC + c + 2)
                for b in range(n + (c == NC - 1)):
                    for s in range(NB):
                        v = win[c][:, s, b, BW:2 * BW] if b < n else v_new[:, s, :]
                        mm = nc.tensor.matmul(o_ps[32 * s:32 * s + 32, :], pT[c % 2][:, b, 32 * s:32 * s + 32], v,
                                              start=(c == 0 and b == 0), stop=(b == n))
                mm.then_inc(s_v, 1)

            with pe.Fori(0, DEC_B // NB) as bt:
                for n in range(2 * NC + 1):
                    if n < 2 * NC:
                        turn_keys(bt, *divmod(n, 2))
                    if n == 1:
                        pe.wait_ge(s_qs, bt + 1)
                    if n > 0:
                        score(bt, *divmod(n - 1, 2))
                turn_probs(bt, 0)
                for c in range(NC):
                    if c < NC - 1:
                        turn_probs(bt, c + 1)
                    times_v(bt, c)

        @block.scalar
        def _(act):
            act.sem_inc(s_kca, 2)
            with act.Fori(0, DEC_B // NB) as bt:
                for c in range(NC):
                    w = chunks[c][2] * P + (NEW if c == NC - 1 else 0)
                    for pair in range(2):
                        act.wait_ge(s_qk, bt * 2 * NC + 2 * c + pair + 1)
                        for s in (0, 2):
                            act.wait_ge(s_kt, bt * 8 * NC + 8 * c + 4 * pair + s + 1)
                            nc.scalar.activation(kT[4 * pair + s][:, 0:w], t_ps[s].rearrange("p a b -> p (a b)")[:, 0:w],
                                                 ACT.Copy).then_inc(s_kca, 1)
                act.wait_ge(s_bias, bt + 1)
                for c in range(NC):
                    cols = s_sb[:, off[c]:off[c] + wide[c]]
                    nc.scalar.activation(cols, cols, ACT.Exp, scale=SCALE, bias=st[:, BIAS:BIAS + 1],
                                         accum_out=den[:, c:c + 1]).then_inc(s_exp, 1)

        @block.vector
        def _(dve):
            dve.sem_inc(s_kcd, 2)
            dve.sem_inc(s_ptc, 1)
            dve.sem_inc(s_sc, 2)
            dve.wait_ge(s_cst, 48)
            dve.wait_ge(s_qt, 1)
            nc.vector.tensor_copy(qT[:, :, :, :].rearrange("p a g t -> p (a g t)"),
                                  p_ps.rearrange("p a b -> p (a b)")[:, 0:2 * NG * NS]).then_inc(s_qtc, 1)
            dve.wait_ge(s_zero, 4)
            dve.wait_ge(s_qtc, 1)
            S = 7
            with dve.Fori(0, DEC_B // NB) as bt:
                for pair in range(2):
                    for hh in range(2):
                        rows, col = slice(E * hh, E * hh + E), (2 * pair + hh) * DEC_T
                        for s in range(NB):
                            ins = nc.vector.tensor_copy(
                                qs[rows, pair, s, :, col:col + DEC_T],
                                qT[rows, pair, :, ds((bt * NB + s) * DEC_T, DEC_T)])
                ins.then_inc(s_qs, 1)

                def scores_in(c):
                    dve.wait_ge(s_qk, bt * 2 * NC + 2 * c + 4)
                    cols = slice(off[c], off[c] + wide[c])
                    nc.vector.tensor_tensor(s_sb[:, cols], s_ps[c % 2][:, 0:wide[c]], mask[:, cols],
                                            ALU.add).then_inc(s_sc, 1)
                    dve.wait_ge(s_sc, bt * NC + c + 3)
                    return nc.vector.tensor_reduce(cmax[:, c:c + 1], s_sb[:, cols], AX.X, ALU.max)
                for c in range(NC):
                    w = chunks[c][2] * P + (NEW if c == NC - 1 else 0)
                    for pair in range(2):
                        dve.wait_ge(s_qk, bt * 2 * NC + 2 * c + pair + 1)
                        for s in (1, 3):
                            dve.wait_ge(s_kt, bt * 8 * NC + 8 * c + 4 * pair + s + 1)
                            nc.vector.tensor_copy(kT[4 * pair + s][:, 0:w],
                                                  t_ps[s].rearrange("p a b -> p (a b)")[:, 0:w]).then_inc(s_kcd, 1)
                    if c > 0:
                        scores_in(c - 1)
                scores_in(NC - 1).then_inc(s_step, 1)
                dve.wait_ge(s_step, bt * S + 1)
                nc.vector.tensor_reduce(st[:, MX:MX + 1], cmax[:, :], AX.X, ALU.max).then_inc(s_step, 1)
                dve.wait_ge(s_step, bt * S + 2)
                nc.vector.tensor_scalar(st[:, BIAS:BIAS + 1], st[:, MX:MX + 1], -SCALE, None,
                                        ALU.mult).then_inc(s_bias, 1)
                for c in range(NC):
                    b = chunks[c][2] + (c == NC - 1)
                    dve.wait_ge(s_pt, bt * NC + c + 1)
                    nc.vector.tensor_copy(pT[c % 2][:, 0:b, :], p_ps[:, 0:b, :]).then_inc(s_ptc, 1)
                nc.vector.tensor_reduce(st[:, SUM:SUM + 1], den[:, :], AX.X, ALU.add).then_inc(s_step, 1)
                dve.wait_ge(s_step, bt * S + 3)
                nc.vector.reciprocal(st[:, REC:REC + 1], st[:, SUM:SUM + 1]).then_inc(s_step, 1)
                dve.wait_ge(s_step, bt * S + 4)
                nc.vector.tensor_scalar(fac[:, :], head[:, :], st[:, REC:REC + 1], None, ALU.mult).then_inc(s_step, 1)
                dve.wait_ge(s_step, bt * S + 5)
                dve.wait_ge(s_v, bt * NC + 2 * NC)
                dve.wait_ge(s_free, bt + 1)
                nc.vector.tensor_scalar(o_sb[:, :], o_ps[:, 0:E], fac[:, 0:1], None, ALU.mult).then_inc(s_step, 1)
                dve.wait_ge(s_step, bt * S + 6)
                for h in range(1, BH):
                    ins = nc.vector.scalar_tensor_tensor(o_sb[:, :], o_ps[:, h * E:(h + 1) * E], fac[:, h:h + 1],
                                                         o_sb[:, :], ALU.mult, ALU.add)
                    if h < BH - 1:
                        ins.then_inc(s_acc, 1)
                        dve.wait_ge(s_acc, bt * (BH - 2) + h)
                    else:
                        ins.then_inc(s_on, 1)
                dve.wait_ge(s_on, bt + 1)
                dve.sem_inc(s_step, 1)


def merge(nc, d, sb, ps, sem, ident, eps, oa, ob, zg, x1d, h2t):
    TILES = NT + 1
    HV = 2 * E
    ctx = ExitStack()
    with ctx:
        raw = sb(ctx, "mg_raw", [P, KT, D])
        wo_hi = sb(ctx, "mg_wo_hi", [P, KT, D], F32R)
        wo_lo = sb(ctx, "mg_wo_lo", [P, KT, D], F32R)
        up = sb(ctx, "mg_up", [P, BW // P, D])
        sub1 = sb(ctx, "mg_sub1", [P, HV])
        subw = sb(ctx, "mg_subw", [P, AH, HV])
        post_g = sb(ctx, "mg_post", [P, D])
        pre_g = sb(ctx, "mg_pre", [P, D])
        oa_sb = [sb(ctx, f"mg_oa{u}", [P, AH, HV]) for u in range(2)]
        g_sb = [sb(ctx, f"mg_g{u}", [P, 2 * D]) for u in range(2)]
        x_sb = [sb(ctx, f"mg_x{u}", [P, D]) for u in range(2)]
        ob_sb = [sb(ctx, f"mg_ob{u}", [P, BW]) for u in range(2)]
        obT = [sb(ctx, f"mg_obT{u}", [P, BW // P, P]) for u in range(2)]
        sq = sb(ctx, "mg_sq", [P, D])
        mT_hi = [sb(ctx, f"mg_mThi{u}", [P, KT, P], F32R) for u in range(1)]
        mT_lo = [sb(ctx, f"mg_mTlo{u}", [P, KT, P], F32R) for u in range(1)]
        y_sb = sb(ctx, "mg_y", [P, D])
        h_sb = [sb(ctx, f"mg_h{u}", [P, D]) for u in range(1)]
        hT_hi = sb(ctx, "mg_hT_hi", [P, KT, P], F32R)
        hT_lo = sb(ctx, "mg_hT_lo", [P, KT, P], F32R)
        SS, RS = 0, AH
        st = [sb(ctx, f"mg_st{u}", [P, 2 * AH + 4]) for u in range(2)]
        Y2, YR, X2, XR = range(2 * AH, 2 * AH + 4)
        up_ps = ps(ctx, "mg_up_ps", [P, D])
        y_ps = ps(ctx, "mg_y_ps", [P, D])
        m_ps = ps(ctx, "mg_m_ps", [P, KT, P])
        h_ps = ps(ctx, "mg_h_ps", [P, KT, P])

        s_w = [sem(f"mg_w{q}") for q in range(KT // 2)]
        s_cst = sem("mg_cst")
        s_whi = sem("mg_whi")
        s_wlo = sem("mg_wlo")
        s_subw = sem("mg_subw_ready")
        s_gin = [sem(f"mg_gin{u}") for u in range(2)]
        s_bin = [sem(f"mg_bin{u}") for u in range(2)]
        s_xin = [sem(f"mg_xin{u}") for u in range(2)]
        s_o = sem("mg_obt")
        s_oc = sem("mg_obtc")
        s_up = sem("mg_uped")
        s_sqa = sem("mg_sqa")
        s_ssa = sem("mg_ssa")
        s_rta = sem("mg_rta")
        s_d1 = sem("mg_d1")
        s_d2 = sem("mg_d2")
        s_m = sem("mg_m")
        s_hi = sem("mg_hi")
        s_lo = sem("mg_lo")
        s_y = sem("mg_yd")
        s_y2 = sem("mg_y2")
        s_d3 = sem("mg_d3")
        s_x2 = sem("mg_x2")
        s_d4 = sem("mg_d4")
        s_h = sem("mg_hd")
        s_hhi = sem("mg_hhi")
        s_hc = sem("mg_hc")
        s_xst = [sem(f"mg_xst{u}") for u in range(2)]
        s_hst = [sem(f"mg_hst{j}") for j in range(2)]
        block = ctx.enter_context(nc.Block())

        def each(eng, step):
            step(-1, 1)
            step(0, 0)
            with eng.Fori(0, 2) as i:
                step(i * 2 + 1, 1)
                step(i * 2 + 2, 0)
            for t in range(5, TILES + 1):
                step(t, t % 2)

        def on(t):
            return not isinstance(t, int) or 0 <= t < TILES

        def rows(tensor, t):
            return tensor[ds(t * P, rows_of(t)), :]

        def got(t, u):
            return (t - u) * 8 + 16

        @block.sync
        def _(sp):
            sp.dma_start(up[:, :, :], d["w_b_up"].rearrange("(k p) n -> p k n", p=P)).then_inc(s_cst, 16)
            sp.dma_start(sub1[:, :], d["subln_w"].to_broadcast([P, HV])).then_inc(s_cst, 16)
            sp.dma_start(post_g[:, :], d["mix_post_norm"].to_broadcast([P, D])).then_inc(s_cst, 16)
            sp.dma_start(pre_g[:, :], d["ffn_pre_norm"].to_broadcast([P, D])).then_inc(s_cst, 16)
            for u in range(2):
                sp.sem_inc(s_xst[u], 16)
            for j in range(2):
                sp.sem_inc(s_hst[j], 16)

            def load_b(t, u, first=False):
                if not first:
                    sp.wait_ge(s_o, t - 1)
                sp.dma_start(ob_sb[u][0:rows_of(t), :], rows(ob, t)).then_inc(s_bin[u], 16)

            def load_g(t, u, first=False):
                if not first:
                    sp.wait_ge(s_m, t - 1)
                r = rows_of(t)
                sp.dma_start(oa_sb[u][0:r, :, :].rearrange("p h e -> p (h e)"), rows(oa, t)).then_inc(s_gin[u], 16)
                sp.dma_start(g_sb[u][0:r, :], rows(zg, t)).then_inc(s_gin[u], 16)

            def load_x(t, u):
                if not isinstance(t, int) or t >= 2:
                    sp.wait_ge(s_d4, t * 2 - 2)
                sp.wait_ge(s_xst[u], (t - u) * 8 + 16)
                sp.dma_start(x_sb[u][0:rows_of(t), :], x_rows(d, t)).then_inc(s_xin[u], 16)

            def step(t, u):
                first = isinstance(t, int) and t < 0
                if first:
                    load_b(0, 0, True)
                    load_b(1, 1, True)
                    load_g(0, 0, True)
                    load_g(1, 1, True)
                    load_x(0, 0)
                    for k in range(0, KT, 2):
                        sp.dma_start(raw[:, k:k + 2, :], d["w_out"].rearrange("(k p) n -> p k n", p=P)[:, k:k + 2, :])\
                          .then_inc(s_w[k // 2], 16)
                if on(t + 3) and (not isinstance(t, int) or t + 3 >= 2):
                    load_b(t + 3, 1 - u)
                if on(t + 1) and not first:
                    load_x(t + 1, 1 - u)
                if on(t + 2) and (not isinstance(t, int) or t + 2 >= 2):
                    load_g(t + 2, u)
                if on(t):
                    sp.wait_ge(s_d3, t * 3 + 3)
                    sp.dma_start(rows(x1d, t), x_sb[u][0:rows_of(t), :]).then_inc(s_xst[u], 16)
            each(sp, step)
            for j in range(2):
                sp.wait_ge(s_hst[j], 16 + 16 * TILES)
            for u in range(2):
                sp.wait_ge(s_xst[u], 16 + 16 * ((TILES + 1 - u) // 2))

        @block.tensor
        def _(pe):
            def turn_b(t, u):
                r = rows_of(t)
                pe.wait_ge(s_bin[u], got(t, u))
                if not isinstance(t, int) or t >= 4:
                    pe.wait_ge(s_hc, t - 3)
                if not isinstance(t, int) or t >= 1:
                    pe.wait_ge(s_oc, t)
                for k in range(BW // P):
                    mm = nc.tensor.transpose(h_ps[:, k, 0:r], ob_sb[u][0:r, k * P:(k + 1) * P], ident[0:r, 0:r])
                mm.then_inc(s_o, 1)

            def up_project(t, u):
                r = rows_of(t)
                pe.wait_ge(s_oc, t + 1)
                if not isinstance(t, int) or t >= 1:
                    pe.wait_ge(s_d2, t * 2 - 1)
                for n in range(D // 512):
                    for k in range(BW // P):
                        mm = nc.tensor.matmul(up_ps[0:r, n * 512:(n + 1) * 512], obT[u][:, k, 0:r],
                                              up[:, k, n * 512:(n + 1) * 512], start=(k == 0), stop=(k == BW // P - 1))
                mm.then_inc(s_up, 1)

            def out_project(t, u):
                r = rows_of(t)
                pe.wait_ge(s_lo, t + 1)
                if not isinstance(t, int) or t >= 1:
                    pe.wait_ge(s_d3, t * 3 - 1)
                for n in range(D // 512):
                    for k in range(KT):
                        if isinstance(t, int) and t == 0 and n == 0 and k % 2 == 0:
                            pe.wait_ge(s_wlo, k // 2 + 1)
                        cols = slice(n * 512, (n + 1) * 512)
                        for j, (a, b) in enumerate(((mT_hi, wo_hi), (mT_lo, wo_hi), (mT_hi, wo_lo))):
                            mm = nc.tensor.matmul(y_ps[0:r, cols], a[0][:, k, 0:r], b[:, k, cols],
                                                  start=(k == 0 and j == 0), stop=(k == KT - 1 and j == 2))
                mm.then_inc(s_y, 1)

            def turn_m(t, u):
                r = rows_of(t)
                pe.wait_ge(s_d2, t * 2 + 2)
                for k in range(KT):
                    mm = nc.tensor.transpose(m_ps[:, k, 0:r], g_sb[u][0:r, k * P:(k + 1) * P], ident[0:r, 0:r])
                mm.then_inc(s_m, 1)

            def turn_h(t, u):
                r = rows_of(t)
                pe.wait_ge(s_d4, t * 2 + 2)
                pe.wait_ge(s_oc, min(t + 4, TILES) if isinstance(t, int) else t + 4)
                for k in range(KT):
                    mm = nc.tensor.transpose(h_ps[:, k, 0:r], h_sb[0][0:r, k * P:(k + 1) * P], ident[0:r, 0:r])
                mm.then_inc(s_h, 1)

            def step(t, u):
                if isinstance(t, int) and t < 0:
                    turn_b(0, 0)
                if on(t + 1):
                    up_project(t + 1, 1 - u)
                if on(t + 2):
                    turn_b(t + 2, u)
                if on(t):
                    out_project(t, u)
                if on(t + 1):
                    turn_m(t + 1, 1 - u)
                if on(t - 1):
                    turn_h(t - 1, 1 - u)
            pe.wait_ge(s_cst, 64)
            each(pe, step)

        @block.scalar
        def _(act):

            def copy_b(t, u):
                r = rows_of(t)
                act.wait_ge(s_o, t + 1)
                if not isinstance(t, int) or t >= 2:
                    act.wait_ge(s_up, t - 1)
                nc.scalar.activation(obT[u][:, :, 0:r], h_ps[:, 0:BW // P, 0:r], ACT.Copy).then_inc(s_oc, 1)

            def root(dst, src, done, n):
                nc.scalar.activation(dst, src, ACT.Sqrt, bias=eps[0:src.shape[0], :]).then_inc(done, n)

            def norm_a(t, u):
                r = rows_of(t)
                act.wait_ge(s_gin[u], (t - u) * 16 + 32)
                nc.scalar.activation(sq[0:r, :], oa_sb[u][0:r, :, :].rearrange("p h e -> p (h e)"), ACT.Square,
                                     scale=HV ** -0.5).then_inc(s_sqa, 1)
                act.wait_ge(s_ssa, t + 1)
                root(st[u][0:r, RS:RS + AH], st[u][0:r, SS:SS + AH], s_rta, 1)

            def split_m(t, u):
                r = rows_of(t)
                act.wait_ge(s_m, t + 1)
                nc.scalar.activation(mT_hi[0][:, :, 0:r], m_ps[:, :, 0:r], ACT.Copy).then_inc(s_hi, 1)

            def norm_y(t, u):
                r = rows_of(t)
                act.wait_ge(s_y, t + 1)
                nc.scalar.activation(sq[0:r, :], y_ps[0:r, :], ACT.Square, scale=D ** -0.5,
                                     accum_out=st[u][0:r, Y2:Y2 + 1]).then_inc(s_y2, 1)
                act.wait_ge(s_y2, t * 2 + 1)
                root(st[u][0:r, YR:YR + 1], st[u][0:r, Y2:Y2 + 1], s_y2, 1)

            def norm_x(t, u):
                r = rows_of(t)
                act.wait_ge(s_d3, t * 3 + 3)
                nc.scalar.activation(sq[0:r, :], x_sb[u][0:r, :], ACT.Square, scale=D ** -0.5,
                                     accum_out=st[u][0:r, X2:X2 + 1]).then_inc(s_x2, 1)
                act.wait_ge(s_x2, t * 2 + 1)
                root(st[u][0:r, XR:XR + 1], st[u][0:r, X2:X2 + 1], s_x2, 1)

            def high_h(t, u):
                r = rows_of(t)
                act.wait_ge(s_h, t + 1)
                act.wait_ge(s_hst[0], t * 16 + 16)
                nc.scalar.activation(hT_hi[:, :, 0:r], h_ps[:, :, 0:r], ACT.Copy).then_inc(s_hhi, 1)
                act.wait_ge(s_hhi, t + 1)
                act.dma_start(h2t[0][:, :, ds(t * P, r)], hT_hi[:, :, 0:r].bitcast(F32)).then_inc(s_hst[0], 16)

            def store_low_h(t, u):
                r = rows_of(t)
                act.wait_ge(s_hc, t + 1)
                act.dma_start(h2t[1][:, :, ds(t * P, r)], hT_lo[:, :, 0:r].bitcast(F32)).then_inc(s_hst[1], 16)

            def step(t, u):
                if isinstance(t, int) and t < 0:
                    copy_b(0, 0)
                if on(t + 1):
                    norm_a(t + 1, 1 - u)
                if on(t + 2):
                    copy_b(t + 2, u)
                if isinstance(t, int) and t < 0:
                    for k in range(0, KT, 2):
                        act.wait_ge(s_w[k // 2], 16)
                        nc.scalar.activation(wo_hi[:, k:k + 2, :], raw[:, k:k + 2, :], ACT.Copy).then_inc(s_whi, 1)
                if on(t + 1):
                    split_m(t + 1, 1 - u)
                if on(t):
                    norm_y(t, u)
                if on(t - 1):
                    high_h(t - 1, 1 - u)
                if on(t):
                    norm_x(t, u)
                if on(t - 1):
                    store_low_h(t - 1, 1 - u)
            each(act, step)

        @block.vector
        def _(dve):
            dve.wait_ge(s_cst, 64)
            nc.vector.tensor_scalar(subw[:, :, :], sub1[:, :].rearrange("p (a e) -> p a e", a=1)
                                    .broadcast_to([P, AH, HV]), 1.0 - LAM_INIT, None, ALU.mult).then_inc(s_subw, 1)
            dve.wait_ge(s_subw, 1)

            def gate_a(t, u):
                r = rows_of(t)
                oat, g = oa_sb[u][0:r, :, :], g_sb[u][0:r, 0:D].rearrange("p (h e) -> p h e", h=AH)
                dve.wait_ge(s_sqa, t + 1)
                nc.vector.tensor_reduce(st[u][0:r, SS:SS + AH], sq[0:r, :].rearrange("p (h e) -> p h e", h=AH), AX.X,
                                        ALU.add).then_inc(s_ssa, 1)
                nc.vector.tensor_tensor(g, g, subw[0:r, :, :], ALU.mult).then_inc(s_d1, 1)
                dve.wait_ge(s_d1, t * 4 + 1)
                nc.vector.tensor_tensor(g, g, oat, ALU.mult).then_inc(s_d1, 1)
                dve.wait_ge(s_rta, t + 1)
                nc.vector.reciprocal(st[u][0:r, RS:RS + AH], st[u][0:r, RS:RS + AH]).then_inc(s_d1, 1)
                dve.wait_ge(s_d1, t * 4 + 3)
                rs = st[u][0:r, RS:RS + AH].unsqueeze(2).broadcast_to([r, AH, HV])
                nc.vector.tensor_tensor(g, g, rs, ALU.mult).then_inc(s_d1, 1)

            def gate_b(t, u):
                r = rows_of(t)
                ga, gb = g_sb[u][0:r, 0:D], g_sb[u][0:r, D:2 * D]
                dve.wait_ge(s_up, t + 1)
                nc.vector.tensor_tensor(gb, gb, up_ps[0:r, :], ALU.mult).then_inc(s_d2, 1)
                dve.wait_ge(s_d1, t * 4 + 4)
                dve.wait_ge(s_d2, t * 2 + 1)
                nc.vector.tensor_tensor(ga, ga, gb, ALU.add).then_inc(s_d2, 1)

            def split_m(t, u):
                r = rows_of(t)
                dve.wait_ge(s_hi, t + 1)
                nc.vector.tensor_tensor(mT_lo[0][:, :, 0:r], m_ps[:, :, 0:r], mT_hi[0][:, :, 0:r].bitcast(F32),
                                        ALU.subtract).then_inc(s_lo, 1)

            def to_x1(t, u):
                r = rows_of(t)
                s = st[u]
                dve.wait_ge(s_y2, t * 2 + 2)
                nc.vector.reciprocal(s[0:r, YR:YR + 1], s[0:r, YR:YR + 1]).then_inc(s_d3, 1)
                dve.wait_ge(s_d3, t * 3 + 1)
                nc.vector.scalar_tensor_tensor(y_sb[0:r, :], y_ps[0:r, :], s[0:r, YR:YR + 1], post_g[0:r, :],
                                               ALU.mult, ALU.mult).then_inc(s_d3, 1)
                dve.wait_ge(s_d3, t * 3 + 2)
                dve.wait_ge(s_xin[u], got(t, u))
                nc.vector.tensor_tensor(x_sb[u][0:r, :], x_sb[u][0:r, :], y_sb[0:r, :], ALU.add).then_inc(s_d3, 1)

            def low_h(t, u):
                r = rows_of(t)
                dve.wait_ge(s_hhi, t + 1)
                dve.wait_ge(s_hst[1], t * 16 + 16)
                nc.vector.tensor_tensor(hT_lo[:, :, 0:r], h_ps[:, :, 0:r], hT_hi[:, :, 0:r].bitcast(F32),
                                        ALU.subtract).then_inc(s_hc, 1)

            def to_h2(t, u):
                r = rows_of(t)
                s = st[u]
                dve.wait_ge(s_x2, t * 2 + 2)
                nc.vector.reciprocal(s[0:r, XR:XR + 1], s[0:r, XR:XR + 1]).then_inc(s_d4, 1)
                dve.wait_ge(s_d4, t * 2 + 1)
                if not isinstance(t, int) or t >= 1:
                    dve.wait_ge(s_h, t)
                nc.vector.scalar_tensor_tensor(h_sb[0][0:r, :], x_sb[u][0:r, :], s[0:r, XR:XR + 1], pre_g[0:r, :],
                                               ALU.mult, ALU.mult).then_inc(s_d4, 1)

            def step(t, u):
                if on(t + 1):
                    gate_a(t + 1, 1 - u)
                    gate_b(t + 1, 1 - u)
                    if isinstance(t, int) and t < 0:
                        for k in range(0, KT, 2):
                            dve.wait_ge(s_whi, k // 2 + 1)
                            nc.vector.tensor_tensor(wo_lo[:, k:k + 2, :], raw[:, k:k + 2, :],
                                                    wo_hi[:, k:k + 2, :].bitcast(F32), ALU.subtract).then_inc(s_wlo, 1)
                    split_m(t + 1, 1 - u)
                if on(t):
                    to_x1(t, u)
                if on(t - 1):
                    low_h(t - 1, 1 - u)
                if on(t):
                    to_h2(t, u)
            each(dve, step)


def ffn(nc, d, sb, ps, sem, eps, x1d, h2t):
    HALVES = ((0, 4, 0), (4, 4, NS))
    MAXT = 4 * P + NS
    ctx = ExitStack()
    with ctx:
        h_hi = sb(ctx, "ff_h_hi", [P, KT, MAXT], F32R)
        h_lo = sb(ctx, "ff_h_lo", [P, KT, MAXT], F32R)
        a_hi = sb(ctx, "ff_a_hi", [P, FB, MAXT], F32R)
        a_lo = sb(ctx, "ff_a_lo", [P, FB, MAXT], F32R)
        UN = 2
        w_raw = [sb(ctx, f"ff_raw{u}", [P, D]) for u in range(UN)]
        w_hi = [sb(ctx, f"ff_whi{u}", [P, D], F32R) for u in range(UN)]
        w_lo = [sb(ctx, f"ff_wlo{u}", [P, D], F32R) for u in range(UN)]
        silu = sb(ctx, "ff_silu", [P, MAXT])
        act_sb = sb(ctx, "ff_act", [P, MAXT])
        post_g = sb(ctx, "ff_post", [P, D])
        y_sb = sb(ctx, "ff_y", [P, 5, D])
        act_y = sb(ctx, "ff_sq", [P, 512], BF16)
        XB = 4
        x_sb = [sb(ctx, f"ff_x{u}", [P, D]) for u in range(XB)]
        st = [sb(ctx, f"ff_st{t}", [P, 5]) for t in range(NT + 1)]
        bank = [ps(ctx, f"ff_b{n}", [P, 512]) for n in range(8)]

        s_cst = sem("ff_cst")
        QP = 4
        s_h = [sem(f"ff_h{q}") for q in range(QP)]
        s_w = [sem(f"ff_w{u}") for u in range(UN)]
        s_whi = sem("ff_whi_made")
        s_wlo = sem("ff_wlo_made")
        s_used = sem("ff_used")
        s_silu = sem("ff_silu_made")
        s_act = sem("ff_act_made")
        s_ahi = sem("ff_ahi_made")
        s_alo = sem("ff_alo_made")
        s_dn = sem("ff_down")
        s_sq = sem("ff_sqd")
        s_dc = sem("ff_downc")
        s_y2 = sem("ff_y2")
        s_d = sem("ff_d")
        s_xin = [sem(f"ff_xin{u}") for u in range(XB)]
        s_yst = [sem(f"ff_yst{u}") for u in range(XB)]
        block = ctx.enter_context(nc.Block())

        GU, DN = 2 * FB, FB
        UH = GU + DN

        def tiles_of(half):
            t0, full, rest = HALVES[half]
            return [(t0 + i, i, P) for i in range(full)] + ([(NT, full, rest)] if rest else [])

        def tokens_of(half):
            return sum(r for _, _, r in tiles_of(half))

        def pieces(half):
            n = tokens_of(half)
            k = -(-n // 512)
            return [(i, n // k) for i in range(k)]

        def out_bank(half, n, i):
            if half == 0:
                return (4 + i, i)[n]
            return ((4, 5, 6, 7, 0), (1, 2, 3, 4, 5))[n][i]

        @block.sync
        def _(sp):
            sp.dma_start(post_g[:, :], d["ffn_post_norm"].to_broadcast([P, D])).then_inc(s_cst, 16)

            def load(U, par, src):
                sp.wait_ge(s_wlo, U + 1)
                sp.dma_start(w_raw[par][:, :], src).then_inc(s_w[par], 16)
            for half in range(2):
                def gate_or_up(j, u):
                    load(half * UH + j * 2 + u, u, d["w_gu"][ds(j, 1), u, :, :].rearrange("a p n -> p (a n)"))
                with sp.Fori(0, FB) as j:
                    for u in range(2):
                        gate_or_up(j, u)
                for n in range(2):
                    for v in range(FB // 2):
                        U = half * UH + GU + n * (FB // 2) + v
                        load(U, U % 2, d["w_down"][n, v, :, :])

        @block.gpsimd
        def _(pool):
            def load_x(k):
                if k >= XB:
                    pool.wait_ge(s_yst[k % XB], 16 * (k // XB))
                t, r = k * P, rows_of(k)
                pool.dma_start(x_sb[k % XB][0:r, :], x1d[t:t + r, :]).then_inc(s_xin[k % XB], 16)

            def store_y(k):
                pool.wait_ge(s_d, k * 3 + 3)
                t, r = (k * P, P) if k < NT else (0, NS)
                out = d["y_prompt"] if k < NT else d["y_sample"]
                pool.dma_start(out[t:t + r, :], x_sb[k % XB][0:r, :]).then_inc(s_yst[k % XB], 16)
            def load_h(half):
                n, t0 = tokens_of(half), HALVES[half][0] * P
                for q in range(QP):
                    for dst, src in ((h_hi, h2t[0]), (h_lo, h2t[1])):
                        pool.dma_start(dst[:, 2 * q:2 * q + 2, 0:n],
                                       src[:, 2 * q:2 * q + 2, t0:t0 + n].bitcast(F32R)).then_inc(s_h[q], 16)
            load_h(0)
            for k in range(XB):
                load_x(k)
            pool.wait_ge(s_used, GU + UN)
            load_h(1)
            for k in range(NT + 1):
                store_y(k)
                if k < NT - XB:
                    load_x(k + XB)
                elif k == NT - XB + 1:
                    load_x(NT)
            for u in range(XB):
                pool.wait_ge(s_yst[u], 16 * ((NT + XB - u) // XB))

        @block.tensor
        def _(pe):
            pe.sem_inc(s_used, UN)

            def gate_up(half, j):
                for u in range(2):
                    U = half * UH + j * 2 + u
                    ps_ = pieces(half)
                    pe.wait_ge(s_wlo, U + 1 + UN)
                    pe.wait_ge(s_silu if u == 0 else s_act, half * FB + j + 1)
                    for x, w in ps_:
                        out = bank[len(ps_) * u + x][:, 0:w]
                        for k in range(KT):
                            if u == 0 and x == 0 and k % 2 == 0:
                                pe.wait_ge(s_h[k // 2], half * 32 + 32)
                            for m, (a, b) in enumerate(((w_hi, h_hi), (w_hi, h_lo), (w_lo, h_hi))):
                                mm = nc.tensor.matmul(out, a[u][:, k * P:(k + 1) * P], b[:, k, x * w:x * w + w],
                                                      start=(k == 0 and m == 0), stop=(k == KT - 1 and m == 2))
                    mm.then_inc(s_used, 1)

            def down(half, n, v):
                U = half * UH + GU + n * (FB // 2) + v
                pe.wait_ge(s_wlo, U + 1 + UN)
                done = half * 8
                for f in range(2):
                    for t, i, r in tiles_of(half):
                        if v == 0 and f == 0 and half == 1 and n == 1 and i >= 3:
                            pe.wait_ge(s_dc, done + i - 2)
                        for m, (a, b) in enumerate(((a_hi, w_hi), (a_lo, w_hi), (a_hi, w_lo))):
                            mm = nc.tensor.matmul(bank[out_bank(half, n, i)][0:r, :],
                                                  a[:, 2 * v + f, i * P:i * P + r], b[U % 2][:, f * 512:(f + 1) * 512],
                                                  start=(v == 0 and f == 0 and m == 0),
                                                  stop=(v == FB // 2 - 1 and f == 1 and m == 2))
                mm.then_inc(s_used, 1)
            for half in range(2):
                if half == 1:
                    pe.wait_ge(s_dc, 8)
                with pe.Fori(0, FB) as j:
                    gate_up(half, j)
                pe.wait_ge(s_alo, (half + 1) * FB + 1)
                for n in range(2):
                    for v in range(FB // 2):
                        down(half, n, v)

        def columns_before(half, n):
            return half * 8 + n * (4 + half)

        def count_w(U, par):
            return (U - par) * 8 + 16

        @block.scalar
        def _(act):
            act.sem_inc(s_silu, 1)
            act.sem_inc(s_ahi, 1)

            def split(U, par):
                act.wait_ge(s_w[par], count_w(U, par))
                act.wait_ge(s_used, U + 1)
                nc.scalar.activation(w_hi[par][:, :], w_raw[par][:, :], ACT.Copy).then_inc(s_whi, 1)

            def square(half, n):
                act.wait_ge(s_used, half * UH + GU + (n + 1) * (FB // 2) + UN)
                for t, i, r in tiles_of(half):
                    nc.scalar.activation(act_y[0:r, :], bank[out_bank(half, n, i)][0:r, :], ACT.Square,
                                         scale=D ** -0.5, accum_out=st[half * 4 + i][0:r, n:n + 1]).then_inc(s_sq, 1)
                    act.wait_ge(s_sq, columns_before(half, n) + i + 1)

            def finish(half):
                for t, i, r in tiles_of(half):
                    k = half * 4 + i
                    act.wait_ge(s_d, k * 3 + 1)
                    nc.scalar.activation(st[k][0:r, 3:4], st[k][0:r, 2:3], ACT.Sqrt, bias=eps[0:r, :]).then_inc(s_y2, 1)
            for half in range(2):
                n = tokens_of(half)
                if half == 0:
                    split(0, 0)
                with act.Fori(0, FB) as j:
                    g = half * FB + j
                    split(half * UH + j * 2 + 1, 1)
                    act.wait_ge(s_used, half * UH + j * 2 + 1 + UN)
                    act.wait_ge(s_act, g + 1)
                    for x, w in pieces(half):
                        ins = nc.scalar.activation(silu[:, x * w:x * w + w], bank[x][:, 0:w], ACT.Silu)
                    ins.then_inc(s_silu, 1)
                    split(half * UH + j * 2 + 2, 0)
                    act.wait_ge(s_act, g + 2)
                    nc.scalar.activation(a_hi[:, ds(j, 1), 0:n].rearrange("p a n -> p (a n)"), act_sb[:, 0:n],
                                         ACT.Copy).then_inc(s_ahi, 1)
                for nn in range(2):
                    for v in range(FB // 2):
                        U = half * UH + GU + nn * (FB // 2) + v
                        if U > half * UH + GU:
                            split(U, U % 2)
                        if nn == 1 and v == 0:
                            square(half, 0)
                if half == 0:
                    split(UH, 0)
                square(half, 1)
                finish(half)

        @block.vector
        def _(dve):
            dve.sem_inc(s_wlo, UN)
            dve.sem_inc(s_act, 1)
            dve.sem_inc(s_alo, 1)
            dve.wait_ge(s_cst, 16)

            def split(U, par):
                dve.wait_ge(s_whi, U + 1)
                nc.vector.tensor_tensor(w_lo[par][:, :], w_raw[par][:, :], w_hi[par][:, :].bitcast(F32),
                                        ALU.subtract).then_inc(s_wlo, 1)

            def columns_out(half, n):
                for t, i, r in tiles_of(half):
                    cols = slice(n * 512, (n + 1) * 512)
                    dve.wait_ge(s_sq, columns_before(half, n) + i + 1)
                    nc.vector.tensor_tensor(y_sb[0:r, i, cols], bank[out_bank(half, n, i)][0:r, :], post_g[0:r, cols],
                                            ALU.mult).then_inc(s_dc, 1)
                    if n == 1:
                        s = st[half * 4 + i]
                        nc.vector.tensor_tensor(s[0:r, 2:3], s[0:r, 0:1], s[0:r, 1:2], ALU.add).then_inc(s_d, 1)
                        finish(half, i, r)

            def finish(half, i, r):
                k = half * 4 + i
                s, x = st[k], x_sb[k % XB]
                dve.wait_ge(s_y2, k + 1)
                nc.vector.reciprocal(s[0:r, 4:5], s[0:r, 3:4]).then_inc(s_d, 1)
                dve.wait_ge(s_d, k * 3 + 2)
                dve.wait_ge(s_dc, columns_before(half, 1) + i + 1)
                dve.wait_ge(s_xin[k % XB], 16 * (k // XB) + 16)
                nc.vector.scalar_tensor_tensor(x[0:r, :], y_sb[0:r, i, :], s[0:r, 4:5], x[0:r, :], ALU.mult,
                                               ALU.add).then_inc(s_d, 1)
            for half in range(2):
                n = tokens_of(half)
                if half == 0:
                    split(0, 0)
                with dve.Fori(0, FB) as j:
                    g = half * FB + j
                    split(half * UH + j * 2 + 1, 1)
                    split(half * UH + j * 2 + 2, 0)
                    dve.wait_ge(s_silu, g + 2)
                    dve.wait_ge(s_used, half * UH + j * 2 + 2 + UN)
                    dve.wait_ge(s_ahi, g + 1)
                    dve.wait_ge(s_alo, g + 1)
                    ps_ = pieces(half)
                    for x, w in ps_:
                        ins = nc.vector.tensor_tensor(act_sb[:, x * w:x * w + w], bank[len(ps_) + x][:, 0:w],
                                                      silu[:, x * w:x * w + w], ALU.mult)
                    ins.then_inc(s_act, 1)
                    dve.wait_ge(s_ahi, g + 2)
                    a = (slice(None), ds(j, 1), slice(0, n))
                    nc.vector.tensor_tensor(a_lo[a].rearrange("p a n -> p (a n)"), act_sb[:, 0:n],
                                            a_hi[a].bitcast(F32).rearrange("p a n -> p (a n)"),
                                            ALU.subtract).then_inc(s_alo, 1)
                for nn in range(2):
                    for v in range(FB // 2):
                        U = half * UH + GU + nn * (FB // 2) + v
                        if U > half * UH + GU:
                            split(U, U % 2)
                        if nn == 1 and v == 0:
                            columns_out(half, 0)
                if half == 0:
                    split(UH, 0)
                columns_out(half, 1)



def _tables():
    bf = mybir.dt.np(BF16)
    f = np.float32
    pos = np.concatenate([np.arange(SEQ), np.tile(PAST + np.arange(DEC_T), DEC_B)]).astype(f)
    inv = np.power(f(THETA), -np.arange(HALF, dtype=f) * f(2.0 / ROT)).astype(f)
    ang = (pos[:, None] * inv[None, :]).astype(f)
    cos, sin = np.cos(ang).astype(f), np.sin(ang).astype(f)

    def tiles(x):
        out = np.zeros(((NT + 1) * P, x.shape[1]), f)
        out[:NTOK] = x
        return np.ascontiguousarray(out.reshape(NT + 1, P, -1).transpose(1, 0, 2))
    c = {"c_ident": np.eye(P, dtype=f), "c_rope_c": tiles(np.concatenate([cos, cos], 1)),
         "c_rope_s": tiles(np.concatenate([-sin, sin], 1))}
    i = np.arange(P)
    c["c_causal"] = np.where(i[None, :] <= i[:, None], 0.0, NEG).astype(bf)
    delta = i[:, None] - i[None, :]
    masks = np.full((P, len(DIL), 3, P), NEG, f)
    for g, dil in enumerate(DIL):
        on = delta % dil == 0
        masks[:, g, 0][on & (delta >= 0)] = 0.0
        masks[:, g, 1][on] = 0.0
        masks[:, g, 2][on & (delta <= 0)] = 0.0
    c["c_dilated"] = masks.astype(bf)
    c["c_new_mask"] = np.where(np.arange(DEC_T)[None, :] <= i[:, None] % DEC_T, 0.0, NEG).astype(f)
    comp = i // DEC_T % 2
    c["c_comp"] = np.stack([comp == 0, comp == 1], 1).astype(f)
    sel = np.zeros((P, 2, NS), f)
    sel[i, i // 16 % 2, i // 16 * DEC_T + i % DEC_T] = 1.0
    c["c_sel"] = sel
    t = i % DEC_T
    cols = []
    for g in (2, 1, 0):
        for j in range(min(DIL[g], DEC_T)):
            on = (t[:, None] % DIL[g] == j) & (DIL[g] * i[None, :] + j >= t[:, None])
            cols.append(on)
    tn = np.arange(DEC_T)
    for g in range(len(DIL)):
        cols.append((tn[None, :] <= t[:, None]) & ((t[:, None] - tn[None, :]) % DIL[g] == 0))
    c["c_win_mask"] = np.where(np.concatenate(cols, 1), 0.0, NEG).astype(f)
    c["c_head"] = (i[:, None] // DEC_T % BH == np.arange(BH)[None, :]).astype(f)
    return c


def _layout(inputs):
    bf = mybir.dt.np(BF16)
    a = {k: np.ascontiguousarray(v) for k, v in inputs.items()}
    w = a["w_in"][0]
    ia = 3 * D
    cols = [w[:, 0:2 * D], w[:, ia:ia + 6 * BW], w[:, 2 * D:3 * D], w[:, ia + 6 * BW:ia + 9 * BW], w[:, ia + 9 * BW:]]
    rot = np.concatenate(cols[0:2], 1)
    val = np.concatenate(cols[2:4], 1)
    val = np.pad(val, ((0, 0), (0, -val.shape[1] % CH)))
    order = np.concatenate([rot[:, :6 * CH], cols[4], rot[:, 6 * CH:], val], 1)
    n = order.shape[1] // CH
    out = {"x_prompt": a["x_prompt"][0], "x_sample": a["x_sample"].reshape(NS, D),
           "w_in": np.ascontiguousarray(order.reshape(KT, P, n, CH).transpose(2, 1, 0, 3)),
           "mix_pre_norm": a["mix_pre_norm"]}
    out["cache_k"] = a["cache_k"][0].reshape(-1, PAGE, D)
    out["cache_v"] = a["cache_v"][0].reshape(-1, PAGE, D)
    out["page_table"] = a["page_table"].reshape(1, -1)
    for g in range(len(WIN)):
        out[f"state_win{g}"] = a[f"state_win{g}"][0].reshape(DEC_B, -1, 2, BW)
    gu = a["w_gu"][0].reshape(KT, P, 2, FB, P)
    out["w_gu"] = np.ascontiguousarray(gu.transpose(3, 2, 1, 0, 4).reshape(FB, 2, P, D))
    down = a["w_down"][0].reshape(FB // 2, 2, P, 2, 512)
    out["w_down"] = np.ascontiguousarray(down.transpose(3, 0, 2, 1, 4).reshape(2, FB // 2, P, D))
    out["w_out"], out["w_b_up"] = a["w_out"][0], a["w_b_up"][0]
    for k in ("subln_w", "mix_post_norm", "ffn_pre_norm", "ffn_post_norm"):
        out[k] = a[k]
    for j in (1, 2):
        out[f"lambda_q{j}"], out[f"lambda_k{j}"] = a[f"lambda_q{j}"], a[f"lambda_k{j}"]
    out.update(_tables())
    out["c_identb"] = np.eye(P, dtype=np.float32).astype(bf)
    return out


_OUTS = [("y_prompt", (SEQ, D), (1, SEQ, D)), ("y_sample", (NS, D), (DEC_B, DEC_T, D)),
         ("new_k_prompt", (SEQ, D), (1, 1, SEQ, AH, 2 * E)), ("new_v_prompt", (SEQ, D), (1, 1, SEQ, AH, 2 * E)),
         ("new_k_sample", (NS, D), (1, DEC_B, DEC_T, AH, 2 * E)),
         ("new_v_sample", (NS, D), (1, DEC_B, DEC_T, AH, 2 * E))]
_OUTS += [(f"new_win{g}_prompt", (min(w, SEQ), 2, BW), (1, 1, min(w, SEQ), 2, BH, E)) for g, w in enumerate(WIN)]
_OUTS += [(f"new_win{g}_sample", (DEC_B, w, 2, BW), (1, DEC_B, w, 2, BH, E)) for g, w in enumerate(WIN)]


def kernel(**inputs):
    import concourse.bacc as _bacc
    from concourse.bass_utils import run_bass_kernel_spmd as _run

    arrays = _layout(inputs)
    nc = _bacc.Bacc("TRN2", target_bir_lowering=False, num_devices=1)
    d = {k: nc.dram_tensor(k, v.shape, mybir.dt.from_np(v.dtype), kind="ExternalInput").ap()
         for k, v in arrays.items()}
    for name, shape, _ in _OUTS:
        d[name] = nc.dram_tensor(name, shape, F32, kind="ExternalOutput").ap()
    build(nc, d)
    r = _run(nc, [arrays], core_ids=[0])
    return tuple(r.results[0][name].reshape(shape) for name, _, shape in _OUTS)
```
